# Optimizing a Trainium2 kernel written in Bass

```python
import math
import jax, jax.numpy as jnp
from jax import lax
import numpy as np

D_MODEL = 1024
BATCH = 1
SEQ = 512
DEPTH = 1

F32 = jnp.float32
CHUNK = 64
N_BRANCH = 4
BRANCH_WIDTH = D_MODEL
EPS = 1e-6

SSM_HEAD_DIM = 64
SSM_HEADS = BRANCH_WIDTH // SSM_HEAD_DIM
SSM_GROUPS = 4
SSM_STATE = 128
SSM_CONV = 4
SSM_XBC = BRANCH_WIDTH + 2 * SSM_GROUPS * SSM_STATE

LRU_BLOCKS = 16
LRU_BLOCK = BRANCH_WIDTH // LRU_BLOCKS
LRU_CONV = 4
LRU_C = 8.0

RET_HEADS = 8
RET_QK_DIM = 64
RET_V_DIM = BRANCH_WIDTH // RET_HEADS
RET_QK = RET_HEADS * RET_QK_DIM
ROPE_BASE = 10000.0

RWKV_HEAD = 64
RWKV_HEADS = BRANCH_WIDTH // RWKV_HEAD
RWKV_W_LORA = 64
RWKV_A_LORA = 64
RWKV_G_LORA = 128
RWKV_IN = 3 * BRANCH_WIDTH + RWKV_W_LORA + RWKV_A_LORA + RWKV_G_LORA
RWKV_LN_EPS = 64e-5

D_FF = 256 * ((8 * D_MODEL // 3 + 255) // 256)
FFN_CONV = 3

IN_SPLITS = (BRANCH_WIDTH, SSM_XBC, SSM_HEADS,
             BRANCH_WIDTH, BRANCH_WIDTH,
             RET_QK, RET_QK, BRANCH_WIDTH, BRANCH_WIDTH,
             RWKV_IN,
             N_BRANCH * D_MODEL)
N_IN = sum(IN_SPLITS)


def rms_norm(x, w):
    xf = x.astype(F32)
    y = xf * lax.rsqrt(jnp.mean(xf * xf, axis=-1, keepdims=True) + EPS)
    return (y * w.astype(F32)).astype(x.dtype)

def head_norm(y, eps):
    mu = jnp.mean(y, axis=-1, keepdims=True)
    yc = y - mu
    return yc * lax.rsqrt(jnp.mean(yc * yc, axis=-1, keepdims=True) + eps)

def causal_dwconv(x, w, b):
    k = w.shape[0]
    y = lax.conv_general_dilated(x, w[:, None, :].astype(x.dtype), window_strides=(1,),
                                 padding=[(k - 1, 0)],
                                 dimension_numbers=('NWC', 'WIO', 'NWC'),
                                 feature_group_count=x.shape[-1])
    return y + b.astype(x.dtype)

def rotary(x, cos, sin):
    x1, x2 = jnp.split(x, 2, axis=-1)
    c, s = cos[:, None, :], sin[:, None, :]
    return jnp.concatenate([x1 * c - x2 * s, x1 * s + x2 * c], axis=-1)

def mamba2_branch(z, xbc, dt, conv_w, conv_b, dt_bias, a_log, d_skip, norm_w):
    b, s, _ = z.shape
    nc, hg = s // CHUNK, SSM_HEADS // SSM_GROUPS
    xbc = jax.nn.silu(causal_dwconv(xbc, conv_w, conv_b)).astype(F32)
    xs, bm, cm = jnp.split(xbc, [BRANCH_WIDTH, BRANCH_WIDTH + SSM_GROUPS * SSM_STATE], axis=-1)
    xs = xs.reshape(b, nc, CHUNK, SSM_GROUPS, hg, SSM_HEAD_DIM)
    bm = bm.reshape(b, nc, CHUNK, SSM_GROUPS, SSM_STATE)
    cm = cm.reshape(b, nc, CHUNK, SSM_GROUPS, SSM_STATE)
    dt = jax.nn.softplus(dt.astype(F32) + dt_bias.astype(F32)).reshape(b, nc, CHUNK, SSM_GROUPS, hg)
    a = -jnp.exp(a_log.astype(F32)).reshape(SSM_GROUPS, hg)
    a_cum = jnp.cumsum(dt * a, axis=2)
    xdt = xs * dt[..., None]
    causal = jnp.tril(jnp.ones((CHUNK, CHUNK), bool))[:, :, None, None]
    seg = a_cum[:, :, :, None] - a_cum[:, :, None, :]
    decay = jnp.exp(jnp.where(causal, seg, -jnp.inf))
    cb = jnp.einsum('bclgn,bcsgn->bclsg', cm, bm)
    y_diag = jnp.einsum('bclsgh,bcsghp->bclghp', cb[..., None] * decay, xdt)
    decay_to_end = jnp.exp(a_cum[:, :, -1:] - a_cum)
    states = jnp.einsum('bclgn,bclgh,bclghp->bcghpn', bm, decay_to_end, xdt)
    chunk_decay = jnp.exp(a_cum[:, :, -1])

    def step(h, inp):
        st, dec = inp
        return h * dec[..., None, None] + st, h

    h0 = jnp.zeros((b, SSM_GROUPS, hg, SSM_HEAD_DIM, SSM_STATE), F32)
    _, prev = lax.scan(step, h0, (jnp.moveaxis(states, 1, 0), jnp.moveaxis(chunk_decay, 1, 0)))
    prev = jnp.moveaxis(prev, 0, 1)
    y_off = jnp.einsum('bclgn,bcghpn,bclgh->bclghp', cm, prev, jnp.exp(a_cum))
    y = y_diag + y_off + xs * d_skip.astype(F32).reshape(SSM_GROUPS, hg, 1)
    y = y.reshape(b, s, BRANCH_WIDTH) * jax.nn.silu(z.astype(F32))
    return rms_norm(y, norm_w).astype(z.dtype)

def rglru_branch(gate_in, x_in, conv_w, conv_b, w_a, b_a, w_i, b_i, lam):
    b, s, _ = x_in.shape
    xc = causal_dwconv(x_in, conv_w, conv_b).astype(F32)
    xb = xc.reshape(b, s, LRU_BLOCKS, LRU_BLOCK)
    r = jax.nn.sigmoid(jnp.einsum('bsgi,gij->bsgj', xb, w_a.astype(F32)).reshape(b, s, BRANCH_WIDTH) + b_a.astype(F32))
    i = jax.nn.sigmoid(jnp.einsum('bsgi,gij->bsgj', xb, w_i.astype(F32)).reshape(b, s, BRANCH_WIDTH) + b_i.astype(F32))
    log_a = -LRU_C * r * jax.nn.softplus(-lam.astype(F32))
    u = jnp.sqrt(-jnp.expm1(2.0 * log_a)) * (i * xc)

    def combine(p, q):
        a1, u1 = p
        a2, u2 = q
        return a1 * a2, a2 * u1 + u2

    _, h = lax.associative_scan(combine, (jnp.exp(log_a), u), axis=1)
    return (h * jax.nn.gelu(gate_in.astype(F32), approximate=True)).astype(x_in.dtype)

def retention_branch(q, k, v, g, norm_w, cos, sin):
    b, s, _ = q.shape
    nc = s // CHUNK
    out_dtype = g.dtype
    qh = rotary(q.astype(F32).reshape(b, s, RET_HEADS, RET_QK_DIM), cos, sin)
    kh = rotary(k.astype(F32).reshape(b, s, RET_HEADS, RET_QK_DIM), cos, sin) * (RET_QK_DIM ** -0.5)
    vh = v.astype(F32).reshape(b, s, RET_HEADS, RET_V_DIM)
    qh, kh, vh = (t.reshape(b, nc, CHUNK, RET_HEADS, t.shape[-1]) for t in (qh, kh, vh))
    log_gamma = jnp.log1p(-jnp.exp2(-5.0 - jnp.arange(RET_HEADS, dtype=F32)))
    pos = jnp.arange(CHUNK, dtype=F32)
    inner = jnp.exp(log_gamma[:, None, None] * jnp.abs(pos[:, None] - pos[None, :]))
    scores = jnp.einsum('bclhd,bcshd->bchls', qh, kh) * inner
    y_inner = jnp.einsum('bchls,bcshe->bclhe', scores, vh)
    k_to_end = jnp.exp(log_gamma[:, None] * (CHUNK - 1.0 - pos))
    kv = jnp.einsum('bcshd,bcshe,hs->bchde', kh, vh, k_to_end)
    chunk_decay = jnp.exp(log_gamma * CHUNK)

    def step(r_state, kv_c):
        return r_state * chunk_decay[:, None, None] + kv_c, r_state

    r0 = jnp.zeros((b, RET_HEADS, RET_QK_DIM, RET_V_DIM), F32)
    _, prev = lax.scan(step, r0, jnp.moveaxis(kv, 1, 0))
    prev = jnp.moveaxis(prev, 0, 1)
    q_from_start = jnp.exp(log_gamma[:, None] * (pos + 1.0))
    y_cross = jnp.einsum('bclhd,bchde,hl->bclhe', qh, prev, q_from_start)
    y = head_norm((y_inner + y_cross).reshape(b, s, RET_HEADS, RET_V_DIM), EPS)
    y = y.reshape(b, s, BRANCH_WIDTH) * norm_w.astype(F32)
    return (jax.nn.silu(g.astype(F32)) * y).astype(out_dtype)

def rwkv7_branch(rw, mu, w0, w2, a0, a2, g2, k_k, k_a, r_k, ln_w, ln_b):
    b, s, _ = rw.shape
    out_dtype = rw.dtype
    rw = rw.astype(F32)
    prev = jnp.pad(rw, ((0, 0), (1, 0), (0, 0)))[:, :-1]
    rw = rw + (prev - rw) * mu.astype(F32)
    wd = BRANCH_WIDTH
    r, k, v, wl, al, gl = jnp.split(
        rw, [wd, 2 * wd, 3 * wd, 3 * wd + RWKV_W_LORA, 3 * wd + RWKV_W_LORA + RWKV_A_LORA], axis=-1)
    w = -jax.nn.softplus(-(w0.astype(F32) + jnp.tanh(wl) @ w2.astype(F32))) - 0.5
    decay = jnp.exp(-jnp.exp(w))
    a = jax.nn.sigmoid(a0.astype(F32) + al @ a2.astype(F32))
    gate = jax.nn.sigmoid(gl) @ g2.astype(F32)
    heads = lambda t: t.reshape(b, s, RWKV_HEADS, RWKV_HEAD)
    kk = heads(k * k_k.astype(F32))
    kk = kk / jnp.maximum(jnp.sqrt(jnp.sum(kk * kk, axis=-1, keepdims=True)), 1e-12)
    k = k * (1.0 + (a - 1.0) * k_a.astype(F32))
    r_h, k_h, v_h, w_h, a_h = heads(r), heads(k), heads(v), heads(decay), heads(a)

    def step(state, inp):
        r_t, w_t, k_t, v_t, kk_t, b_t = inp
        sk = jnp.einsum('bhvk,bhk->bhv', state, kk_t)
        state = (state * w_t[:, :, None, :] - sk[..., None] * b_t[:, :, None, :]
                 + v_t[..., None] * k_t[:, :, None, :])
        return state, jnp.einsum('bhvk,bhk->bhv', state, r_t)

    s0 = jnp.zeros((b, RWKV_HEADS, RWKV_HEAD, RWKV_HEAD), F32)
    seq_first = lambda t: jnp.moveaxis(t, 1, 0)
    _, o = lax.scan(step, s0, (seq_first(r_h), seq_first(w_h), seq_first(k_h), seq_first(v_h),
                               seq_first(kk), seq_first(kk * a_h)))
    o = jnp.moveaxis(o, 0, 1)
    o = head_norm(o, RWKV_LN_EPS).reshape(b, s, wd) * ln_w.astype(F32) + ln_b.astype(F32)
    bonus = jnp.sum(r_h * k_h * r_k.astype(F32).reshape(RWKV_HEADS, RWKV_HEAD), axis=-1, keepdims=True) * v_h
    o = o + bonus.reshape(b, s, wd)
    return (o * gate).astype(out_dtype)

def hybrid_mixer(h, w_in, ssm_p, lru_p, ret_p, rwkv_p, w_branch, w_out, cos, sin):
    b, s, _ = h.shape
    proj = h @ w_in
    (m_z, m_xbc, m_dt, l_gate, l_x, r_q, r_k, r_v, r_g, rw, gate_logits) = jnp.split(
        proj, np.cumsum(IN_SPLITS)[:-1].tolist(), axis=-1)
    y_ssd = mamba2_branch(m_z, m_xbc, m_dt, *ssm_p)
    y_lru = rglru_branch(l_gate, l_x, *lru_p)
    y_ret = retention_branch(r_q, r_k, r_v, r_g, *ret_p, cos, sin)
    y_rwkv = rwkv7_branch(rw, *rwkv_p)
    ys = jnp.stack([y_ssd, y_lru, y_ret, y_rwkv], axis=2)
    branch = jnp.einsum('bsmw,mwd->bsmd', ys, w_branch)
    gates = jax.nn.sigmoid(gate_logits.astype(F32)).reshape(b, s, N_BRANCH, D_MODEL)
    merged = jnp.sum(gates * branch.astype(F32), axis=2).astype(h.dtype)
    return merged @ w_out

def conv_ffn(h, w_up, conv_w, conv_b, w_down):
    u = causal_dwconv(h @ w_up, conv_w, conv_b)
    val, gt = jnp.split(u, 2, axis=-1)
    return (jax.nn.silu(gt) * val) @ w_down

def first_inputs(seed: int = 0) -> dict:
    key = jax.random.key(seed)
    ks = iter(jax.random.split(key, 64))
    nrm = lambda shape, scale: jax.random.normal(next(ks), shape, F32) * scale
    unif = lambda shape, lo, hi: jax.random.uniform(next(ks), shape, F32, lo, hi)
    L, W, D = DEPTH, BRANCH_WIDTH, D_MODEL
    gain = lambda shape: 1.0 + nrm(shape, 0.02)
    x = nrm((BATCH, SEQ, D), 1.0)
    norm_mix = gain((L, D))
    w_in = nrm((L, D, N_IN), D ** -0.5)
    ssm_conv_w = nrm((L, SSM_CONV, SSM_XBC), SSM_CONV ** -0.5)
    ssm_conv_b = nrm((L, SSM_XBC), 0.02)
    dt0 = jnp.exp(unif((L, SSM_HEADS), math.log(1e-3), math.log(1e-1)))
    ssm_dt_bias = dt0 + jnp.log(-jnp.expm1(-dt0))
    ssm_a_log = jnp.log(unif((L, SSM_HEADS), 1.0, 16.0))
    ssm_d = 1.0 + nrm((L, SSM_HEADS), 0.1)
    ssm_norm = gain((L, W))
    lru_conv_w = nrm((L, LRU_CONV, W), LRU_CONV ** -0.5)
    lru_conv_b = nrm((L, W), 0.02)
    lru_w_a = nrm((L, LRU_BLOCKS, LRU_BLOCK, LRU_BLOCK), LRU_BLOCK ** -0.5)
    lru_b_a = nrm((L, W), 0.02)
    lru_w_i = nrm((L, LRU_BLOCKS, LRU_BLOCK, LRU_BLOCK), LRU_BLOCK ** -0.5)
    lru_b_i = nrm((L, W), 0.02)
    p = unif((L, W), 0.9, 0.999) ** (1.0 / LRU_C)
    lru_lam = jnp.log(p) - jnp.log1p(-p)
    ret_norm = gain((L, W))
    rwkv_mu = unif((L, RWKV_IN), 0.0, 1.0)
    ratio = jnp.arange(W, dtype=F32) / (W - 1)
    rwkv_w0 = (-7.0 + 5.0 * ratio ** 0.85 + 0.5)[None, :] + nrm((L, W), 0.1)
    rwkv_w2 = nrm((L, RWKV_W_LORA, W), 0.1 * RWKV_W_LORA ** -0.5)
    rwkv_a0 = nrm((L, W), 0.1)
    rwkv_a2 = nrm((L, RWKV_A_LORA, W), 0.5 * RWKV_A_LORA ** -0.5)
    rwkv_g2 = nrm((L, RWKV_G_LORA, W), RWKV_G_LORA ** -0.5)
    rwkv_k_k = 0.85 + nrm((L, W), 0.02)
    rwkv_k_a = 1.0 + nrm((L, W), 0.02)
    rwkv_r_k = nrm((L, W), 0.1)
    rwkv_ln_w = gain((L, W))
    rwkv_ln_b = nrm((L, W), 0.02)
    w_branch = nrm((L, N_BRANCH, W, D), W ** -0.5)
    w_out = nrm((L, D, D), D ** -0.5)
    norm_ffn = gain((L, D))
    ffn_up = nrm((L, D, 2 * D_FF), D ** -0.5)
    ffn_conv_w = nrm((L, FFN_CONV, 2 * D_FF), FFN_CONV ** -0.5)
    ffn_conv_b = nrm((L, 2 * D_FF), 0.02)
    ffn_down = nrm((L, D_FF, D), D_FF ** -0.5)
    norm_final = gain((D,))
    return {"x": x, "norm_mix": norm_mix, "w_in": w_in,
            "ssm_conv_w": ssm_conv_w, "ssm_conv_b": ssm_conv_b, "ssm_dt_bias": ssm_dt_bias,
            "ssm_a_log": ssm_a_log, "ssm_d": ssm_d, "ssm_norm": ssm_norm,
            "lru_conv_w": lru_conv_w, "lru_conv_b": lru_conv_b, "lru_w_a": lru_w_a,
            "lru_b_a": lru_b_a, "lru_w_i": lru_w_i, "lru_b_i": lru_b_i, "lru_lam": lru_lam,
            "ret_norm": ret_norm,
            "rwkv_mu": rwkv_mu, "rwkv_w0": rwkv_w0, "rwkv_w2": rwkv_w2, "rwkv_a0": rwkv_a0,
            "rwkv_a2": rwkv_a2, "rwkv_g2": rwkv_g2, "rwkv_k_k": rwkv_k_k, "rwkv_k_a": rwkv_k_a,
            "rwkv_r_k": rwkv_r_k, "rwkv_ln_w": rwkv_ln_w, "rwkv_ln_b": rwkv_ln_b,
            "w_branch": w_branch, "w_out": w_out, "norm_ffn": norm_ffn,
            "ffn_up": ffn_up, "ffn_conv_w": ffn_conv_w, "ffn_conv_b": ffn_conv_b,
            "ffn_down": ffn_down, "norm_final": norm_final}

def first_block(x, norm_mix, w_in, ssm_conv_w, ssm_conv_b, ssm_dt_bias, ssm_a_log, ssm_d, ssm_norm,
              lru_conv_w, lru_conv_b, lru_w_a, lru_b_a, lru_w_i, lru_b_i, lru_lam, ret_norm,
              rwkv_mu, rwkv_w0, rwkv_w2, rwkv_a0, rwkv_a2, rwkv_g2, rwkv_k_k, rwkv_k_a, rwkv_r_k,
              rwkv_ln_w, rwkv_ln_b, w_branch, w_out, norm_ffn, ffn_up, ffn_conv_w, ffn_conv_b,
              ffn_down, norm_final):
    s = x.shape[1]
    pos = jnp.arange(s, dtype=F32)
    inv_freq = ROPE_BASE ** (-jnp.arange(0, RET_QK_DIM, 2, dtype=F32) / RET_QK_DIM)
    ang = pos[:, None] * inv_freq[None, :]
    cos, sin = jnp.cos(ang), jnp.sin(ang)
    for l in range(DEPTH):
        h = rms_norm(x, norm_mix[l])
        ssm_p = (ssm_conv_w[l], ssm_conv_b[l], ssm_dt_bias[l], ssm_a_log[l], ssm_d[l], ssm_norm[l])
        lru_p = (lru_conv_w[l], lru_conv_b[l], lru_w_a[l], lru_b_a[l], lru_w_i[l], lru_b_i[l], lru_lam[l])
        ret_p = (ret_norm[l],)
        rwkv_p = (rwkv_mu[l], rwkv_w0[l], rwkv_w2[l], rwkv_a0[l], rwkv_a2[l], rwkv_g2[l],
                  rwkv_k_k[l], rwkv_k_a[l], rwkv_r_k[l], rwkv_ln_w[l], rwkv_ln_b[l])
        x = x + hybrid_mixer(h, w_in[l], ssm_p, lru_p, ret_p, rwkv_p, w_branch[l], w_out[l], cos, sin)
        h = rms_norm(x, norm_ffn[l])
        x = x + conv_ffn(h, ffn_up[l], ffn_conv_w[l], ffn_conv_b[l], ffn_down[l])
    return rms_norm(x, norm_final)


_first_inputs = first_inputs


def first_inputs(seed=0):
    import zlib

    import numpy as np

    out = dict(_first_inputs(seed))
    spreads = {}
    factors = {'ssm_conv_b': 4.399,
     'ssm_norm': 88.219,
     'lru_b_a': 200.0,
     'lru_b_i': 200.0,
     'ret_norm': 138.656,
     'rwkv_w2': 8.0,
     'rwkv_a0': 4.889,
     'rwkv_k_k': 200.0,
     'rwkv_k_a': 98.337,
     'rwkv_ln_w': 149.257,
     'rwkv_ln_b': 165.213,
     'norm_ffn': 14.252,
     'ffn_conv_b': 14.698,
     'norm_final': 25.651,
     'lru_conv_b': 51.144,
     'lru_w_a': 23.752,
     'lru_lam': 23.72,
     'lru_conv_w': 8.0,
     'lru_w_i': 8.0}
    for name, (base, spread) in spreads.items():
        noise = np.random.default_rng([zlib.crc32(name.encode()), seed]).standard_normal(out[name].shape)
        drawn = base * np.exp(spread * noise) if base else spread * noise
        out[name] = __import__('jax').numpy.asarray(drawn.astype(out[name].dtype))
    for name, factor in factors.items():
        out[name] = (out[name] * factor).astype(out[name].dtype)
    return out


_narrow_inputs = first_inputs


def first_inputs(seed=0):

    out = dict(_narrow_inputs(seed))
    wider = {'ssm_norm': 4.21,
     'ret_norm': 4.22,
     'rwkv_k_k': 5.85,
     'rwkv_ln_w': 4.22,
     'rwkv_ln_b': 4.24,
     'norm_final': 3.32}
    for name, times in wider.items():
        mean = out[name].mean()
        out[name] = (mean + times * (out[name] - mean)).astype(out[name].dtype)
    return out


CTX_LEN = 256
GRID_W = 64

GDN_HEADS = 4
GDN_HEAD_DIM = 128
GDN_WIDTH = GDN_HEADS * GDN_HEAD_DIM
CONV_W = 5

NA_HEADS = 8
NA_HEAD_DIM = 64
NA_WIDTH = NA_HEADS * NA_HEAD_DIM
NA_ROWS = 8
NA_COLS = 16

MIX_WIDTH = GDN_WIDTH + NA_WIDTH
IN_COLS = 4 * GDN_WIDTH + 4 * GDN_HEADS + 3 * NA_WIDTH

N_EXPERTS = 16
CAPACITY_FACTOR = 2
D_EXPERT = 1024


def rms_norm_2(x, w):
    xf = x.astype(jnp.float32)
    y = xf * lax.rsqrt(jnp.mean(xf * xf, axis=-1, keepdims=True) + EPS)
    return y.astype(x.dtype) * w

def l2_normalize(t):
    tf = t.astype(jnp.float32)
    return (tf * lax.rsqrt(jnp.sum(tf * tf, axis=-1, keepdims=True) + EPS)).astype(t.dtype)

def modulate(h, shift, scale):
    return h * (1.0 + scale) + shift

def depthwise_conv(x, w):
    C = x.shape[-1]
    return lax.conv_general_dilated(
        x, w[:, None, :].astype(x.dtype), window_strides=(1,),
        padding=((CONV_W // 2, CONV_W // 2),),
        dimension_numbers=('NWC', 'WIO', 'NWC'), feature_group_count=C)

def axial_rope(x):
    T, D = x.shape[1], x.shape[-1]
    half = D // 2
    pairs = half // 2
    t = jnp.arange(T)
    inv_freq = ROPE_BASE ** (-jnp.arange(pairs, dtype=jnp.float32) / pairs)

    def rot(xa, pos):
        ang = pos.astype(jnp.float32)[:, None] * inv_freq[None, :]
        cos = jnp.cos(ang)[None, :, None, :].astype(x.dtype)
        sin = jnp.sin(ang)[None, :, None, :].astype(x.dtype)
        x1, x2 = xa[..., :pairs], xa[..., pairs:]
        return jnp.concatenate([x1 * cos - x2 * sin, x2 * cos + x1 * sin], axis=-1)

    return jnp.concatenate([rot(x[..., :half], t // GRID_W), rot(x[..., half:], t % GRID_W)], axis=-1)

def gdn_inputs(p_qkv, p_a, p_b, conv_w, a_log, dt_bias, rotary):
    B, T, _ = p_qkv.shape
    qkv = jax.nn.silu(depthwise_conv(p_qkv, conv_w))
    q, k, v = jnp.split(qkv, 3, axis=-1)
    heads = lambda t: t.reshape(B, T, GDN_HEADS, GDN_HEAD_DIM)
    q, k, v = l2_normalize(heads(q)), l2_normalize(heads(k)), heads(v)
    if rotary:
        q, k = axial_rope(q), axial_rope(k)
    a = p_a.astype(jnp.float32).reshape(B, T, 2, GDN_HEADS)
    b = p_b.astype(jnp.float32).reshape(B, T, 2, GDN_HEADS)
    g = -jnp.exp(a_log.astype(jnp.float32)) * jax.nn.softplus(a + dt_bias.astype(jnp.float32))
    beta = jax.nn.sigmoid(b)
    return q, k, v, g, beta

def chunk_gated_delta(q, k, v, g, beta, s0):
    B, H, T, dk = k.shape
    dv = v.shape[-1]
    n = T // CHUNK
    q = q * (dk ** -0.5)
    q, k, v = [t.reshape(B, H, n, CHUNK, t.shape[-1]) for t in (q, k, v)]
    g = g.reshape(B, H, n, CHUNK)
    beta = beta.reshape(B, H, n, CHUNK)
    gcum = jnp.cumsum(g, axis=-1)
    incl = jnp.tril(jnp.ones((CHUNK, CHUNK), dtype=bool))
    strict = jnp.tril(jnp.ones((CHUNK, CHUNK), dtype=bool), -1)
    decay = jnp.exp(jnp.where(incl, gcum[..., :, None] - gcum[..., None, :], -jnp.inf))
    kb = k * beta[..., None]
    lower = jnp.where(strict, jnp.einsum('bhnid,bhnjd->bhnij', kb, k) * decay, 0.0)
    eye = jnp.eye(CHUNK, dtype=jnp.float32)
    tinv = lax.linalg.triangular_solve(eye + lower, jnp.broadcast_to(eye, lower.shape),
                                       left_side=True, lower=True, unit_diagonal=True)
    u = tinv @ (v * beta[..., None])
    w = tinv @ (kb * jnp.exp(gcum)[..., None])
    attn = jnp.where(incl, jnp.einsum('bhnid,bhnjd->bhnij', q, k) * decay, 0.0)
    q_dec = q * jnp.exp(gcum)[..., None]
    k_dec = k * jnp.exp(gcum[..., -1:] - gcum)[..., None]
    g_last = jnp.exp(gcum[..., -1])
    xs = tuple(jnp.moveaxis(t, 2, 0) for t in (q_dec, k_dec, u, w, attn, g_last))

    def step(S, inp):
        qd, kd, ui, wi, ai, gl = inp
        v_new = ui - wi @ S
        o = qd @ S + ai @ v_new
        S = S * gl[..., None, None] + jnp.einsum('bhcd,bhce->bhde', kd, v_new)
        return S, o

    S, o = lax.scan(step, s0, xs)
    return jnp.moveaxis(o, 0, 2).reshape(B, H, T, dv), S

def bidirectional_gated_delta(lat, cin):
    q, k, v, g, beta = lat
    qc, kc, vc, gc, bc = cin
    B = q.shape[0]
    bhtd = lambda t: jnp.swapaxes(t, 1, 2).astype(jnp.float32)
    bht = lambda t, d: jnp.swapaxes(t[:, :, d, :], 1, 2).astype(jnp.float32)
    s0 = jnp.zeros((B, GDN_HEADS, GDN_HEAD_DIM, GDN_HEAD_DIM), jnp.float32)
    outs_l, outs_c = [], []
    for d in range(2):
        order = (lambda t: jnp.flip(t, axis=2)) if d == 1 else (lambda t: t)
        oc, s_ctx = chunk_gated_delta(order(bhtd(qc)), order(bhtd(kc)), order(bhtd(vc)),
                                      order(bht(gc, d)), order(bht(bc, d)), s0)
        ol, _ = chunk_gated_delta(order(bhtd(q)), order(bhtd(k)), order(bhtd(v)),
                                  order(bht(g, d)), order(bht(beta, d)), s_ctx)
        outs_l.append(order(ol))
        outs_c.append(order(oc))
    o_l = jnp.swapaxes(outs_l[0] + outs_l[1], 1, 2).astype(q.dtype)
    o_c = jnp.swapaxes(outs_c[0] + outs_c[1], 1, 2).astype(q.dtype)
    return o_l, o_c

def gated_rms_norm(o, gate, w):
    B, T, H, dv = o.shape
    y = rms_norm_2(o, w) * jax.nn.silu(gate.reshape(B, T, H, dv))
    return y.reshape(B, T, H * dv)

def neighbourhood_attention(q, k, v, kc, vc, rpb):
    B, T, H, dh = q.shape
    rows = T // GRID_W
    win_rows = min(NA_ROWS, rows)
    grid = lambda t: t.reshape(B, rows, GRID_W, H, dh)
    qg, kg, vg = grid(q * (dh ** -0.5)), grid(k), grid(v)
    col = jnp.arange(GRID_W)
    col_start = jnp.clip(col - NA_COLS // 2, 0, GRID_W - NA_COLS)
    col_in = (col[None, :] >= col_start[:, None]) & (col[None, :] < col_start[:, None] + NA_COLS)
    col_idx = jnp.clip(col[None, :] - col[:, None], -(NA_COLS - 1), NA_COLS - 1) + (NA_COLS - 1)
    rpb_f = rpb.astype(jnp.float32)
    n_lat = win_rows * GRID_W

    def row_block(r):
        start = jnp.clip(r - win_rows // 2, 0, rows - win_rows)
        kr = lax.dynamic_slice_in_dim(kg, start, win_rows, axis=1)
        vr = lax.dynamic_slice_in_dim(vg, start, win_rows, axis=1)
        qr = lax.dynamic_index_in_dim(qg, r, axis=1, keepdims=False)
        row_idx = start + jnp.arange(win_rows) - r + (NA_ROWS - 1)
        bias = rpb_f[:, row_idx][:, :, col_idx].transpose(0, 2, 1, 3)
        s_lat = jnp.einsum('bqhd,brkhd->bhqrk', qr, kr).astype(jnp.float32) + bias[None]
        s_lat = jnp.where(col_in[:, None, :], s_lat, -jnp.inf)
        s_ctx = jnp.einsum('bqhd,bchd->bhqc', qr, kc).astype(jnp.float32)
        s = jnp.concatenate([s_lat.reshape(B, H, GRID_W, n_lat), s_ctx], axis=-1)
        p = jax.nn.softmax(s, axis=-1).astype(q.dtype)
        p_lat = p[..., :n_lat].reshape(B, H, GRID_W, win_rows, GRID_W)
        p_ctx = p[..., n_lat:]
        return (jnp.einsum('bhqrk,brkhd->bqhd', p_lat, vr)
                + jnp.einsum('bhqc,bchd->bqhd', p_ctx, vc))

    out = lax.map(row_block, jnp.arange(rows))
    return jnp.moveaxis(out, 0, 1).reshape(B, T, H * dh)

def context_attention(qc, kc, vc):
    B, Tc, H, dh = qc.shape
    s = jnp.einsum('bqhd,bkhd->bhqk', qc * (dh ** -0.5), kc).astype(jnp.float32)
    p = jax.nn.softmax(s, axis=-1).astype(qc.dtype)
    return jnp.einsum('bhqk,bkhd->bqhd', p, vc).reshape(B, Tc, H * dh)

def token_mixer(h, hc, w_in, conv_qkv, a_log, dt_bias, gdn_norm, na_rpb, w_out, need_ctx):
    B, T, _ = h.shape
    Tc = hc.shape[1]
    cuts = (3 * GDN_WIDTH, 4 * GDN_WIDTH, 4 * GDN_WIDTH + 2 * GDN_HEADS, 4 * GDN_WIDTH + 4 * GDN_HEADS)
    qkv, gate, a, b, na = jnp.split(h @ w_in, cuts, axis=-1)
    qkv_c, gate_c, a_c, b_c, na_c = jnp.split(hc @ w_in, cuts, axis=-1)
    lat = gdn_inputs(qkv, a, b, conv_qkv, a_log, dt_bias, True)
    cin = gdn_inputs(qkv_c, a_c, b_c, conv_qkv, a_log, dt_bias, False)
    o_gdn, o_gdn_c = bidirectional_gated_delta(lat, cin)
    y_gdn = gated_rms_norm(o_gdn, gate, gdn_norm)
    na_heads = lambda t, n: t.reshape(B, n, 3, NA_HEADS, NA_HEAD_DIM)
    nl = na_heads(na, T)
    ncx = na_heads(na_c, Tc)
    y_na = neighbourhood_attention(nl[:, :, 0], nl[:, :, 1], nl[:, :, 2], ncx[:, :, 1], ncx[:, :, 2], na_rpb)
    y = jnp.concatenate([y_gdn, y_na], axis=-1) @ w_out
    if not need_ctx:
        return y, None
    y_c_gdn = gated_rms_norm(o_gdn_c, gate_c, gdn_norm)
    y_c_na = context_attention(ncx[:, :, 0], ncx[:, :, 1], ncx[:, :, 2])
    y_c = jnp.concatenate([y_c_gdn, y_c_na], axis=-1) @ w_out
    return y, y_c

def expert_choice_ffn(h, w_router, w_gate, w_up, w_down):
    B, T, D = h.shape
    cap = CAPACITY_FACTOR * T // N_EXPERTS
    aff = jax.nn.softmax((h @ w_router).astype(jnp.float32), axis=-1)
    gval, idx = lax.top_k(jnp.swapaxes(aff, 1, 2), cap)
    xe = jax.vmap(lambda hb, ib: hb[ib])(h, idx)
    hid = jax.nn.silu(jnp.einsum('becd,edf->becf', xe, w_gate)) * jnp.einsum('becd,edf->becf', xe, w_up)
    ye = jnp.einsum('becf,efd->becd', hid, w_down) * gval[..., None].astype(h.dtype)
    return jax.vmap(lambda yb, ib: jnp.zeros((T, D), yb.dtype).at[ib.reshape(-1)].add(yb.reshape(-1, D)))(ye, idx)

def second_inputs(seed: int = 0) -> dict:
    key = jax.random.key(seed)
    ks = jax.random.split(key, 20)
    f32 = jnp.float32
    nrm = lambda k, shape, s: jax.random.normal(k, shape, f32) * s
    D = D_MODEL
    dt = jnp.exp(jax.random.uniform(ks[11], (DEPTH, 2, GDN_HEADS), f32, math.log(1e-3), math.log(1e-1)))
    return {
        'x': nrm(ks[0], (BATCH, SEQ, D), 1.0),
        'c': nrm(ks[1], (BATCH, D), 1.0),
        'ctx': nrm(ks[2], (BATCH, CTX_LEN, D), 1.0),
        'c_ctx': nrm(ks[3], (D,), 1.0),
        'w_mod': nrm(ks[4], (DEPTH, D, 6 * D), 0.5 * D ** -0.5),
        'b_mod': nrm(ks[5], (DEPTH, 6 * D), 0.02),
        'norm_mix': 1.0 + nrm(ks[6], (DEPTH, D), 0.1),
        'norm_ffn': 1.0 + nrm(ks[7], (DEPTH, D), 0.1),
        'w_in': nrm(ks[8], (DEPTH, D, IN_COLS), D ** -0.5),
        'conv_qkv': nrm(ks[9], (DEPTH, CONV_W, 3 * GDN_WIDTH), CONV_W ** -0.5),
        'a_log': jnp.log(jax.random.uniform(ks[10], (DEPTH, 2, GDN_HEADS), f32, 1.0, 16.0)),
        'dt_bias': dt + jnp.log(-jnp.expm1(-dt)),
        'gdn_norm': 1.0 + nrm(ks[12], (DEPTH, GDN_HEAD_DIM), 0.1),
        'na_rpb': nrm(ks[13], (DEPTH, NA_HEADS, 2 * NA_ROWS - 1, 2 * NA_COLS - 1), 0.2),
        'w_out': nrm(ks[14], (DEPTH, MIX_WIDTH, D), MIX_WIDTH ** -0.5),
        'w_router': nrm(ks[15], (DEPTH, D, N_EXPERTS), D ** -0.5),
        'w_gate': nrm(ks[16], (DEPTH, N_EXPERTS, D, D_EXPERT), D ** -0.5),
        'w_up': nrm(ks[17], (DEPTH, N_EXPERTS, D, D_EXPERT), D ** -0.5),
        'w_down': nrm(ks[18], (DEPTH, N_EXPERTS, D_EXPERT, D), D_EXPERT ** -0.5),
        'final_norm': 1.0 + nrm(ks[19], (D,), 0.1),
    }

def second_block(x, c, ctx, c_ctx, w_mod, b_mod, norm_mix, norm_ffn, w_in, conv_qkv, a_log, dt_bias,
              gdn_norm, na_rpb, w_out, w_router, w_gate, w_up, w_down, final_norm):
    for li in range(DEPTH):
        need_ctx = li + 1 < DEPTH
        mod = jax.nn.silu(c) @ w_mod[li] + b_mod[li]
        mod_c = jax.nn.silu(c_ctx) @ w_mod[li] + b_mod[li]
        sh1, sc1, gt1, sh2, sc2, gt2 = jnp.split(mod[:, None, :], 6, axis=-1)
        sh1c, sc1c, gt1c, sh2c, sc2c, gt2c = jnp.split(mod_c, 6, axis=-1)
        h = modulate(rms_norm_2(x, norm_mix[li]), sh1, sc1)
        hc = modulate(rms_norm_2(ctx, norm_mix[li]), sh1c, sc1c)
        y, y_c = token_mixer(h, hc, w_in[li], conv_qkv[li], a_log[li], dt_bias[li], gdn_norm[li],
                             na_rpb[li], w_out[li], need_ctx)
        x = x + gt1 * y
        h2 = modulate(rms_norm_2(x, norm_ffn[li]), sh2, sc2)
        x = x + gt2 * expert_choice_ffn(h2, w_router[li], w_gate[li], w_up[li], w_down[li])
        if need_ctx:
            ctx = ctx + gt1c * y_c
            hc2 = modulate(rms_norm_2(ctx, norm_ffn[li]), sh2c, sc2c)
            ctx = ctx + gt2c * expert_choice_ffn(hc2, w_router[li], w_gate[li], w_up[li], w_down[li])
    return rms_norm_2(x, final_norm)


def setup_inputs(seed=0):
    out = dict(first_inputs(seed))
    for name, value in second_inputs(seed + 1).items():
        if name != "x":
            out[name + "_2"] = value
    return out


def reference(
    x, norm_mix, w_in, ssm_conv_w, ssm_conv_b, ssm_dt_bias, ssm_a_log, ssm_d, ssm_norm,
    lru_conv_w, lru_conv_b, lru_w_a, lru_b_a, lru_w_i, lru_b_i, lru_lam, ret_norm, rwkv_mu,
    rwkv_w0, rwkv_w2, rwkv_a0, rwkv_a2, rwkv_g2, rwkv_k_k, rwkv_k_a, rwkv_r_k, rwkv_ln_w,
    rwkv_ln_b, w_branch, w_out, norm_ffn, ffn_up, ffn_conv_w, ffn_conv_b, ffn_down, norm_final,
    c_2, ctx_2, c_ctx_2, w_mod_2, b_mod_2, norm_mix_2, norm_ffn_2, w_in_2, conv_qkv_2, a_log_2,
    dt_bias_2, gdn_norm_2, na_rpb_2, w_out_2, w_router_2, w_gate_2, w_up_2, w_down_2,
    final_norm_2,
):
    x = first_block(
        x, norm_mix, w_in, ssm_conv_w, ssm_conv_b, ssm_dt_bias, ssm_a_log, ssm_d, ssm_norm,
        lru_conv_w, lru_conv_b, lru_w_a, lru_b_a, lru_w_i, lru_b_i, lru_lam, ret_norm, rwkv_mu,
        rwkv_w0, rwkv_w2, rwkv_a0, rwkv_a2, rwkv_g2, rwkv_k_k, rwkv_k_a, rwkv_r_k, rwkv_ln_w,
        rwkv_ln_b, w_branch, w_out, norm_ffn, ffn_up, ffn_conv_w, ffn_conv_b, ffn_down,
        norm_final,
    )
    return second_block(
        x, c_2, ctx_2, c_ctx_2, w_mod_2, b_mod_2, norm_mix_2, norm_ffn_2, w_in_2, conv_qkv_2,
        a_log_2, dt_bias_2, gdn_norm_2, na_rpb_2, w_out_2, w_router_2, w_gate_2, w_up_2,
        w_down_2, final_norm_2,
    )


_drawn_inputs = setup_inputs


def setup_inputs(seed=0):
    import zlib

    import numpy as np

    out = dict(_drawn_inputs(seed))
    spreads = {}
    factors = {'c_2': 8.0,
     'ctx_2': 8.0,
     'c_ctx_2': 8.0,
     'w_mod_2': 8.0,
     'b_mod_2': 8.0,
     'norm_mix_2': 8.0,
     'norm_ffn_2': 8.0,
     'w_in_2': 8.0,
     'conv_qkv_2': 8.0,
     'a_log_2': 8.0,
     'dt_bias_2': 8.0,
     'gdn_norm_2': 8.0,
     'na_rpb_2': 8.0,
     'w_out_2': 8.0,
     'w_router_2': 8.0,
     'w_gate_2': 8.0,
     'w_up_2': 8.0,
     'w_down_2': 8.0}
    for name, (base, spread) in spreads.items():
        noise = np.random.default_rng([zlib.crc32(name.encode()), seed]).standard_normal(out[name].shape)
        drawn = base * np.exp(spread * noise) if base else spread * noise
        out[name] = __import__('jax').numpy.asarray(drawn.astype(out[name].dtype))
    for name, factor in factors.items():
        out[name] = (out[name] * factor).astype(out[name].dtype)
    return out
```

```python
from contextlib import ExitStack

import numpy as np
import concourse.bass as bass
from concourse import mybir

F32 = mybir.dt.float32
ALU = mybir.AluOpType
ACT = mybir.ActivationFunctionType
AX = mybir.AxisListType

P = 128
D = 1024
KT = D // P
T = 512
TT = T // P
EPS = 1e-6
CHUNK = 64
FF = 2816
FT = FF // P
CTX = 256

PLANES = 87
H_PL = 0
MRG_PL = 8
RING_PL = 16
RING = 6
WORK = RING_PL + 2 * RING
PAIRS = 8

W_Z, W_XBC, W_LG, W_LX, W_RQ, W_RK, W_RV, W_RG, W_RW, W_GATE = 0, 8, 24, 32, 40, 44, 48, 56, 64, 90

COLS = [("norm_mix", 8), ("ssm_conv_w", 64), ("ssm_conv_b", 16), ("ssm_norm", 8), ("ssm_d", 8),
        ("lru_conv_w", 32), ("lru_conv_b", 8), ("lru_b_a", 8), ("lru_b_i", 8), ("lru_lam", 8),
        ("ret_norm", 8), ("rwkv_mu", 26), ("rwkv_w0", 8), ("rwkv_a0", 8), ("rwkv_k_k", 8),
        ("rwkv_k_a", 8), ("rwkv_r_k", 8), ("rwkv_ln_w", 8), ("rwkv_ln_b", 8), ("norm_ffn", 8),
        ("ffn_conv_w", 132), ("ffn_conv_b", 44), ("norm_final", 8),
        ("c_2", 8), ("c_ctx_2", 8), ("b_mod_2", 48), ("norm_mix_2", 8), ("norm_ffn_2", 8),
        ("conv_qkv_2", 60), ("gdn_norm_2", 1), ("final_norm_2", 8),
        ("ssm_dt_bias", 1), ("ssm_a_log", 1), ("gdn_a_log", 8), ("gdn_dt_bias", 8)]
COL_AT = {}
_n = 0
for _name, _k in COLS:
    COL_AT[_name] = _n
    _n += _k
NCOLS = _n

CONSTS = [("ident", 128), ("ones", 128), ("causal", 128), ("headsum", 128), ("iota", 128),
          ("sel", 16 * 128), ("rot", 128), ("chunkstart", 512),
          ("pairsel", 1024), ("onecol", 15), ("paircol", 30),
          ("strict", 128), ("incl", 128), ("level", 6 * 128), ("levelT", 6 * 128),
          ("strictT", 128), ("inclT", 128), ("flip", 128), ("every16", 128)]
CONST_AT = {}
_n = 0
for _name, _k in CONSTS:
    CONST_AT[_name] = _n
    _n += _k
NCONST = _n


def consts():
    c = np.zeros((P, NCONST), np.float32)

    def put(name, a):
        c[:a.shape[0], CONST_AT[name]:CONST_AT[name] + a.shape[1]] = a

    i = np.arange(P)
    put("ident", np.eye(P))
    put("ones", np.ones((P, P)))
    put("causal", (i[:, None] <= i[None, :]).astype(np.float32))
    put("headsum", (i[:, None] // 64 == i[None, :] // 64).astype(np.float32))
    put("iota", np.tile(i.astype(np.float32), (P, 1)))
    sel = np.zeros((16, 16, P), np.float32)
    sel[np.arange(16), np.arange(16), :] = 1.0
    put("sel", sel.reshape(16, -1))
    rot = np.zeros((P, P), np.float32)
    for b in (0, 64):
        for d in range(32):
            rot[b + 32 + d, b + d] = -1.0
            rot[b + d, b + 32 + d] = 1.0
    put("rot", rot)
    start = np.ones((P, T), np.float32)
    start[:, ::CHUNK] = 0.0
    put("chunkstart", start)
    pair = np.zeros((16, 8, P), np.float32)
    for ch in range(8):
        pair[2 * ch, ch, :64] = 1.0
        pair[2 * ch + 1, ch, 64:] = 1.0
    put("pairsel", pair.reshape(16, -1))
    one = np.zeros((P, 15), np.float32)
    one[:, 7] = 1.0
    put("onecol", one)
    two = np.zeros((P, 30), np.float32)
    two[:64, 14] = 1.0
    two[64:, 15] = 1.0
    put("paircol", two)
    r, c2 = i[:, None], i[None, :]
    same = r // CHUNK == c2 // CHUNK
    put("strict", ((r < c2) & same).astype(np.float32))
    put("incl", ((r <= c2) & same).astype(np.float32))
    lev = [((c2 >> n) % 2 == 1) & (r >> n == (c2 >> n) - 1) for n in range(6)]
    put("level", np.concatenate(lev, axis=1).astype(np.float32))
    put("levelT", np.concatenate([m.T for m in lev], axis=1).astype(np.float32))
    put("strictT", ((r > c2) & same).astype(np.float32))
    put("inclT", ((r >= c2) & same).astype(np.float32))
    put("flip", np.eye(P)[::-1])
    put("every16", np.tile((i % 16 != 0).astype(np.float32), (P, 1)))
    return c


def ret_tables():
    lg = np.log1p(-np.exp2(-5.0 - np.arange(8)))
    s = np.arange(P)[:, None]
    l = np.arange(T)[None, :]
    seen = (s // CHUNK <= l // CHUNK)
    m = np.exp(lg[:, None, None] * np.abs(l - s)[None]) * seen[None]
    pos = np.arange(T)[None, :]
    inv = 10000.0 ** (-np.arange(0, 64, 2) / 64.0)
    ang = (pos * inv[:, None].astype(np.float32)).astype(np.float32)
    cos = np.tile(np.cos(ang), (4, 1))
    sin = np.tile(np.sin(ang), (4, 1))
    return np.ascontiguousarray(m.transpose(1, 0, 2)).astype(np.float32), cos.astype(np.float32), sin.astype(np.float32)


class Chain:

    def __init__(self, sem):
        self.sem, self.n = sem, 0

    def __call__(self, eng, ins):
        self.n += 1
        ins.then_inc(self.sem, 1)
        eng.wait_ge(self.sem, self.n)


class Core:

    def __init__(self, nc, ctx, dram):
        self.nc, self.ctx, self.dram = nc, ctx, dram
        self.phases = None
        self.arena = self.sb("arena", PLANES * T)
        self.params = self.sb("params", NCOLS)
        self.cst = self.sb("cst", NCONST)
        self.small = self.sb("small", 256)
        self.mods = self.sb("mods", 160)
        self.ps = ctx.enter_context(nc.psum_tensor("ps", [P, 8, 512], F32))
        self.loaded = [self.sem(f"loaded{i}") for i in range(RING)]
        self.piece_done = self.sem("piece_done")
        self.pieces = 0
        self.ahead = 0
        self.plan, self.planned = [], 0
        self.act_evac = self.sem("act_evac")
        self.dve_evac = self.sem("dve_evac")
        self.conv_done = self.sem("conv_done")
        self.post_done = self.sem("post_done")
        self.n_act = self.n_dve = self.n_conv = self.n_post = 0
        self.dve_chain = Chain(self.sem("dve_chain"))
        self.act_chain = Chain(self.sem("act_chain"))
        self.pool_chain = Chain(self.sem("pool_chain"))
        self.rms = [self.sem(f"rms_{s}") for s in ("squared", "summed", "inverse", "root")]
        self.n_rms = 0
        self.out_done = self.sem("out_done")
        self.recycle()

    def sb(self, name, n):
        return self.ctx.enter_context(self.nc.sbuf_tensor(name, [P, n], F32))

    def sem(self, name):
        s = (self.phases or self.ctx).enter_context(self.nc.semaphore(name))
        if self.phases:
            self.used.append(s)
        return s

    def recycle(self):
        if self.phases and self.used:
            with self.nc.Block() as block:
                @block.gpsimd
                def _(pool):
                    for s in self.used:
                        pool.sem_clear(s)
            self.phases.close()
        self.phases, self.used = self.ctx.enter_context(ExitStack()), []

    def pl(self, i, n=1):
        return self.arena[:, i * T:(i + n) * T]

    def col(self, name, i=0, n=1):
        a = COL_AT[name] + i
        return self.params[:, a:a + n]

    def const(self, name, n=None):
        a = CONST_AT[name]
        return self.cst[:, a:a + (n or dict(CONSTS)[name])]

    def bank(self, b):
        return self.ps[:, b, :]


def load_phase(k, moves, done=None):
    done = done or k.sem(f"moved{k.nc.next_id()}")
    with k.nc.Block() as block:
        @block.sync
        def _(sp):
            for dst, src in moves:
                sp.dma_start(dst, src).then_inc(done, 16)
            sp.wait_ge(done, 16 * len(moves))


def plan(k, step, *args, ring=False, **more):
    k.plan.append((step, args, more, ring))


def run_plan(k):
    for n, (step, args, more, _) in enumerate(k.plan):
        if step is project_phase or step is experts_phase:
            following = []
            for later, a, _, ring in k.plan[n + 1:]:
                if ring:
                    break
                if later is project_phase:
                    following = [p[0] for j in a[1] for p in j["pieces"]][:RING]
                    break
                if later is experts_phase:
                    following = [k.dram["w_gate"][0, q * P:(q + 1) * P, :] for q in range(RING)]
                    break
            more = dict(more, following=following)
        step(*args, **more)
    k.plan.clear()


def load_following(k, sp, following):
    for i, src in enumerate(following):
        g = k.pieces_end + i
        if g >= RING:
            sp.wait_ge(k.piece_done, g - RING + 1)
        sp.dma_start(k.pl(RING_PL + 2 * (g % RING), 2)[:, :src.shape[-1]], src).then_inc(k.loaded[g % RING], 16)


def job(pieces, rhs, eng, dst, m=P, n=T, **more):
    return dict(pieces=pieces, rhs=rhs, eng=eng, dst=dst, m=m, n=n, **more)


def wtile(w, i, kt=KT):
    return [(w[i, :, a * P:min(a + 8, kt) * P], a, min(8, kt - a)) for a in range(0, kt, 8)]


def project_phase(k, jobs, following=(), beside=None):
    nc = k.nc
    piece0, a0, d0, c0, q0 = k.pieces, k.n_act, k.n_dve, k.n_conv, k.n_post
    last_piece, evac, na, nd, nconv, npost, np_ = [], [], 0, 0, 0, 0, 0
    for j in jobs:
        np_ += len(j["pieces"])
        last_piece.append(piece0 + np_)
        if j["eng"] == "A":
            na += 1
            evac.append((k.act_evac, a0 + na))
        else:
            nd += 1
            evac.append((k.dve_evac, d0 + nd))
        if j.get("post"):
            nconv += 1
            j["conv_n"] = c0 + nconv
        if j.get("post") or j.get("signal"):
            npost += 1
            j["post_n"] = q0 + npost
        if j.get("needs") is not None:
            j["needs_n"] = jobs[j["needs"]]["post_n"]
    pieces = [p for j in jobs for p in j["pieces"]]
    k.pieces_end = piece0 + np_
    BANKS = 6

    def slot(g):
        return k.pl(RING_PL + 2 * (g % RING), 2)

    with nc.Block() as block:
        @block.sync
        def _(sp):
            for i, (src, _, kn) in enumerate(pieces):
                g = piece0 + i
                if i < k.ahead:
                    continue
                if g >= RING:
                    sp.wait_ge(k.piece_done, g - RING + 1)
                sp.dma_start(slot(g)[:, :src.shape[-1]], src).then_inc(k.loaded[g % RING], 16)
            load_following(k, sp, following)

        if beside is not None:
            block.gpsimd(beside)

        @block.tensor
        def _(pe):
            g = piece0
            for i, j in enumerate(jobs):
                if i >= BANKS:
                    pe.wait_ge(*evac[i - BANKS])
                out = k.bank(i % BANKS)
                kt = sum(p[2] for p in j["pieces"])
                for src, ka, kn in j["pieces"]:
                    pe.wait_ge(k.loaded[g % RING], 16 * (g // RING + 1))
                    w = slot(g)
                    m = src.shape[-1] // kn
                    if j.get("swap"):
                        for t in range(j["n"] // P):
                            for q in range(kn):
                                last = nc.tensor.matmul(out[:, t * m:(t + 1) * m], j["rhs"](ka + q)[:, t * P:(t + 1) * P],
                                                        w[:, q * m:(q + 1) * m], start=(q == 0), stop=(q == kn - 1))
                    else:
                        for q in range(kn):
                            last = nc.tensor.matmul(out[0:m, 0:j["n"]], w[:, q * m:(q + 1) * m], j["rhs"](ka + q),
                                                    start=(ka + q == 0), stop=(ka + q == kt - 1))
                    last.then_inc(k.piece_done, 1)
                    g += 1

        @block.scalar
        def _(act):
            for i, j in enumerate(jobs):
                if j["eng"] == "A":
                    act.wait_ge(k.piece_done, last_piece[i])
                    src = k.bank(i % BANKS)[0:j["m"], 0:j["n"]]
                    if j.get("swap"):
                        src = k.bank(i % BANKS)[:, 0:j["n"] // P * j["m"]].rearrange("p (t m) -> p t m", m=j["m"])
                    for lo, hi, func in j.get("parts", [(0, j["m"], j.get("func", ACT.Copy))]):
                        s, o = (src, j["dst"]) if hi - lo == P or j.get("swap") else (src[lo:hi, :], j["dst"][lo:hi, :])
                        if j.get("bias") is not None:
                            ins = nc.scalar.activation(o, s, func, bias=j["bias"])
                        else:
                            ins = nc.scalar.activation(o, s, func)
                    ins.then_inc(k.act_evac, 1)
                    if j.get("signal"):
                        act.wait_ge(k.act_evac, evac[i][1])
                        nc.scalar.nop().then_inc(k.post_done, 1)
                elif j.get("post"):
                    act.wait_ge(k.conv_done, j["conv_n"])
                    ps = j["post"]
                    for n, (lo, hi, func) in enumerate(ps):
                        ins = nc.scalar.activation(j["dst"][lo:hi, :], j["dst"][lo:hi, :], func)
                    ins.then_inc(k.post_done, 1)

        @block.vector
        def _(dve):
            link = lambda ins: k.dve_chain(dve, ins)
            for i, j in enumerate(jobs):
                if j["eng"] != "D":
                    continue
                dve.wait_ge(k.piece_done, last_piece[i])
                src, dst, n = k.bank(i % BANKS)[0:j["m"], 0:j["n"]], j["dst"], j["n"]
                if j.get("taps"):
                    c, sh = j["taps"][0]
                    if j.get("bias") is not None:
                        ins = nc.vector.tensor_scalar(dst, src, c, j["bias"], ALU.mult, ALU.add)
                    else:
                        ins = nc.vector.tensor_scalar(dst, src, c, None, ALU.mult)
                    for c, sh in j["taps"][1:]:
                        link(ins)
                        o, s = (dst[:, sh:n], src[:, 0:n - sh]) if sh > 0 else (dst[:, 0:n + sh], src[:, -sh:n])
                        ins = nc.vector.scalar_tensor_tensor(out=o, in0=s, scalar=c, in1=o, op0=ALU.mult, op1=ALU.add)
                    ins.then_inc(k.dve_evac, 1)
                    if j.get("post"):
                        dve.wait_ge(k.dve_evac, evac[i][1])
                        nc.vector.engine_nop().then_inc(k.conv_done, 1)
                    if j.get("mul") is not None:
                        dve.wait_ge(k.dve_evac, evac[i][1])
                        dve.wait_ge(k.post_done, j["needs_n"])
                        link(nc.vector.tensor_tensor(j["mul"], j["mul"], dst, ALU.mult))
                elif j.get("gate") is not None:
                    dve.wait_ge(k.post_done, j["needs_n"])
                    if j["first"]:
                        nc.vector.tensor_tensor(dst, src, j["gate"], ALU.mult).then_inc(k.dve_evac, 1)
                    else:
                        nc.vector.tensor_tensor(j["gate"], src, j["gate"], ALU.mult).then_inc(k.dve_evac, 1)
                        dve.wait_ge(k.dve_evac, evac[i][1])
                        link(nc.vector.tensor_tensor(dst, dst, j["gate"], ALU.add))
                elif j.get("times") is not None:
                    nc.vector.tensor_tensor(dst, src, j["times"], ALU.mult).then_inc(k.dve_evac, 1)
                elif j.get("scale") is not None:
                    nc.vector.scalar_tensor_tensor(out=dst, in0=src, scalar=j["scale"], in1=j["add"], op0=ALU.mult,
                                                   op1=ALU.add).then_inc(k.dve_evac, 1)
                else:
                    nc.vector.tensor_tensor(dst, src, j["add"], ALU.add).then_inc(k.dve_evac, 1)

    k.pieces += np_
    k.ahead = len(following)
    k.n_act += na
    k.n_dve += nd
    k.n_conv += nconv
    k.n_post += npost


def rms_phase(k, src, dst, weight, scratch, n=T, shift=None):
    nc = k.nc
    squared, summed, inverse, root = k.rms
    b = k.n_rms
    k.n_rms += 1
    sq = lambda c: k.pl(scratch + c)[:, 0:n]
    inv, rt = k.pl(scratch + KT)[:, 0:n], k.pl(scratch + KT + 1)[:, 0:n]
    with nc.Block() as block:
        @block.scalar
        def _(act):
            for c in range(KT):
                nc.scalar.activation(sq(c), src(c), ACT.Square).then_inc(squared, 1)
            act.wait_ge(inverse, b + 1)
            nc.scalar.activation(rt, inv, ACT.Sqrt).then_inc(root, 1)

        @block.tensor
        def _(pe):
            for c in range(KT):
                pe.wait_ge(squared, b * KT + c + 1)
                last = nc.tensor.matmul(k.bank(0)[:, 0:n], k.const("ones"), sq(c), start=(c == 0), stop=(c == KT - 1))
            last.then_inc(summed, 1)

        @block.vector
        def _(dve):
            link = lambda ins: k.dve_chain(dve, ins)
            dve.wait_ge(summed, b + 1)
            link(nc.vector.tensor_scalar(inv, k.bank(0)[:, 0:n], 1.0 / D, EPS, ALU.mult, ALU.add))
            nc.vector.reciprocal(inv, inv).then_inc(inverse, 1)
            dve.wait_ge(root, b + 1)
            for c in range(KT):
                ins = nc.vector.scalar_tensor_tensor(out=dst(c), in0=src(c), scalar=weight(c), in1=rt, op0=ALU.mult,
                                                     op1=ALU.mult)
                link(ins)
                if shift is not None:
                    link(nc.vector.tensor_scalar(dst(c), dst(c), shift(c), None, ALU.add))


def softplus_steps(k, dve, act, x, y, z, w, e_done, e_ready, base, pre=None):
    nc = k.nc
    link = lambda ins: k.dve_chain(dve, ins)
    link(nc.vector.tensor_scalar(y, x, -1.0, None, ALU.mult))
    link(nc.vector.tensor_tensor(y, x, y, ALU.min))
    nc.vector.tensor_scalar(x, x, 0.0, None, ALU.max).then_inc(e_ready, 1)
    dve.wait_ge(e_done, base + 1)
    link(nc.vector.tensor_scalar(w, z, 2.0, None, ALU.add))
    link(nc.vector.reciprocal(w, w))
    link(nc.vector.tensor_tensor(z, z, w, ALU.mult))
    link(nc.vector.tensor_tensor(w, z, z, ALU.mult))
    link(nc.vector.tensor_scalar(y, w, 1.0 / 15, 1.0 / 13, ALU.mult, ALU.add))
    for d in (11, 9, 7, 5, 3, 1):
        link(nc.vector.tensor_tensor(y, y, w, ALU.mult))
        link(nc.vector.tensor_scalar(y, y, 1.0 / d, None, ALU.add))
    link(nc.vector.tensor_tensor(y, y, z, ALU.mult))
    link(nc.vector.scalar_tensor_tensor(out=x, in0=y, scalar=2.0, in1=x, op0=ALU.mult, op1=ALU.add))


OFF = [0, 512, 896, 1152]
TRI = 1280


def tri_bank(k, s, i):
    n = T - P * i
    return k.ps[:, 3 * s + (0, 1, 2, 2)[i], (0, 0, 0, 256)[i]:(0, 0, 0, 256)[i] + n]


def mamba_phase(k, z, xs, bt, ct, dt, w):
    nc = k.nc
    y0, xdt0, cb0, e0 = w, w + 8, w + 16, MRG_PL
    rel = k.pl(w + 27, 3)[0:16, 0:TRI]
    sp_ = [k.pl(w + 30 + i)[0:16, :] for i in range(4)]
    dta = k.pl(w + 21)[0:16, :]
    colr = k.small[:, 0:64].rearrange("p (i h) -> p i h", h=16)
    dtc = k.small[:, 64:128].rearrange("p (i h) -> p i h", h=16)
    nega = k.small[0:16, 128:129]
    x = k.pl(dt)[0:16, :]
    cb = lambda g: k.pl(cb0, 5)[:, (g % 2) * TRI:(g % 2) * TRI + TRI]
    ee = lambda h: k.pl(e0, 8)[:, (h % 3) * TRI:(h % 3) * TRI + TRI]
    xdt = k.pl(xdt0, 8).rearrange("p (i c) -> p i c", c=D)
    order = []
    for h in range(16):
        if h % 4 == 0:
            order.append(("cb", h // 4))
        order.append(("r", h))
    freed, cnt = [], {"cb": 0, "r": 0}
    for kind, _ in order:
        cnt[kind] += 1
        freed.append((kind, cnt[kind]))
    e_ready, e_done, dt_in = k.sem("m_e_ready"), k.sem("m_e_done"), k.sem("m_dt_in")
    rel_ok, small_t, small_ok = k.sem("m_rel_ok"), k.sem("m_small_t"), k.sem("m_small_ok")
    xs_t, xdt_ok = k.sem("m_xs_t"), k.sem("m_xdt_ok")
    tri_ok, cb_copied, sub_ok = k.sem("m_tri_ok"), k.sem("m_cb_copied"), k.sem("m_sub_ok")
    exp_ok, mult_ok, y_ok, y_out = k.sem("m_exp_ok"), k.sem("m_mult_ok"), k.sem("m_y_ok"), k.sem("m_y_out")

    with nc.Block() as block:
        @block.scalar
        def _(act):
            nc.scalar.activation(nega, k.col("ssm_a_log")[0:16, :], ACT.Exp).then_inc(dt_in, 1)
            act.wait_ge(e_ready, 1)
            nc.scalar.activation(sp_[1], sp_[0], ACT.Exp).then_inc(e_done, 1)
            for j in range(17):
                if j < 16 and j % 4 == 0:
                    g = j // 4
                    act.wait_ge(tri_ok, 5 * g + 1)
                    if g >= 2:
                        act.wait_ge(mult_ok, 4 * (g - 1))
                    for i, wd in ((0, 512), (1, 384), (2, 384)):
                        ins = nc.scalar.activation(cb(g)[:, OFF[i]:OFF[i] + wd], k.ps[:, 3 * ((5 * g) % 2) + i, 0:wd], ACT.Copy)
                    ins.then_inc(cb_copied, 1)
                if j < 16:
                    act.wait_ge(sub_ok, j + 1)
                    nc.scalar.activation(ee(j), ee(j), ACT.Exp).then_inc(exp_ok, 1)

        @block.tensor
        def _(pe):
            pe.wait_ge(rel_ok, 1)
            for i in range(TT):
                nc.tensor.transpose(k.bank(6)[:, 16 * i:16 * i + 16], rel[:, OFF[i]:OFF[i] + P], k.const("ident")[0:16, 0:16])
            for i in range(TT):
                ins = nc.tensor.transpose(k.bank(6)[:, 64 + 16 * i:80 + 16 * i], x[:, i * P:(i + 1) * P], k.const("ident")[0:16, 0:16])
            ins.then_inc(small_t, 1)
            for n in range(8):
                i, half = n // 2, n % 2
                if n >= 2:
                    pe.wait_ge(xdt_ok, n - 1)
                for c in range(4):
                    ins = nc.tensor.transpose(k.bank(n % 2)[:, c * P:(c + 1) * P], k.pl(xs + 4 * half + c)[:, i * P:(i + 1) * P], k.const("ident"))
                ins.then_inc(xs_t, 1)
            pe.wait_ge(xdt_ok, 8)
            for n in range(len(order) + 2):
                if n < len(order):
                    kind, h = order[n]
                    if n >= 2:
                        fk, fn = freed[n - 2]
                        pe.wait_ge(cb_copied if fk == "cb" else sub_ok, fn)
                    for i in range(TT):
                        out = tri_bank(k, n % 2, i)
                        if kind == "cb":
                            ins = nc.tensor.matmul(out, k.pl(bt + h)[:, i * P:(i + 1) * P], k.pl(ct + h)[:, i * P:T], start=True, stop=True)
                        else:
                            ins = nc.tensor.matmul(out, k.const("sel")[0:16, h * P:(h + 1) * P], rel[:, OFF[i]:OFF[i] + T - P * i], start=True, stop=True)
                    ins.then_inc(tri_ok, 1)
                if n >= 2 and order[n - 2][0] == "r":
                    h = order[n - 2][1]
                    pe.wait_ge(mult_ok, h + 1)
                    if h % 2 == 0 and h >= 4:
                        pe.wait_ge(y_out, h // 2 - 1)
                    lo = 64 * (h % 2)
                    out = k.bank(6 + (h // 2) % 2)[lo:lo + 64, :]
                    for i in range(TT):
                        ins = nc.tensor.matmul(out[:, i * P:T], xdt[:, i, h * 64:h * 64 + 64], ee(h)[:, OFF[i]:OFF[i] + T - P * i], start=(i == 0), stop=(i == 3))
                    ins.then_inc(y_ok, 1)

        @block.vector
        def _(dve):
            link = lambda ins: k.dve_chain(dve, ins)
            link(nc.vector.tensor_scalar(x, x, k.col("ssm_dt_bias")[0:16, :], None, ALU.add))
            softplus_steps(k, dve, None, x, sp_[0], sp_[1], sp_[2], e_done, e_ready, 0)
            dve.wait_ge(dt_in, 1)
            link(nc.vector.tensor_scalar(nega, nega, -1.0, None, ALU.mult))
            link(nc.vector.tensor_scalar(dta, x, nega, None, ALU.mult))
            link(nc.vector.memset(sp_[3], 1.0))
            for i in range(TT):
                n = T - P * i
                link(nc.vector.tensor_tensor_scan(rel[:, OFF[i]:OFF[i] + n], sp_[3][:, 0:n], dta[:, P * i:T], 0.0, ALU.mult, ALU.add))
            nc.vector.engine_nop().then_inc(rel_ok, 1)
            dve.wait_ge(small_t, 1)
            link(nc.vector.tensor_scalar(k.small[:, 0:64], k.bank(6)[:, 0:64], -1.0, None, ALU.mult))
            link(nc.vector.tensor_copy(k.small[:, 64:128], k.bank(6)[:, 64:128]))
            for n in range(8):
                i, half = n // 2, n % 2
                dve.wait_ge(xs_t, n + 1)
                o = xdt[:, i, half * 512:half * 512 + 512].rearrange("p (h d) -> p h d", d=64)
                s = k.bank(n % 2).rearrange("p (h d) -> p h d", d=64)
                nc.vector.tensor_tensor(o, s, dtc[:, i, 8 * half:8 * half + 8].unsqueeze(2).broadcast_to([P, 8, 64]), ALU.mult).then_inc(xdt_ok, 1)
            for j in range(16 + 4):
                if j < 16 and j % 4 == 0:
                    dve.wait_ge(cb_copied, j // 4 + 1)
                    for i in range(TT):
                        d = cb(j // 4)[:, OFF[i]:OFF[i] + P]
                        link(nc.vector.tensor_tensor(d, d, k.const("causal"), ALU.mult))
                if j < 16:
                    h = j
                    dve.wait_ge(tri_ok, 5 * (h // 4) + 2 + h % 4)
                    if h >= 3:
                        dve.wait_ge(y_ok, h - 2)
                    for i in range(TT):
                        n = T - P * i
                        s = (5 * (h // 4) + 1 + h % 4) % 2
                        ins = nc.vector.tensor_scalar(ee(h)[:, OFF[i]:OFF[i] + n], tri_bank(k, s, i), colr[:, i, h:h + 1], 0.0, ALU.add, ALU.min)
                    ins.then_inc(sub_ok, 1)
                if 1 <= j <= 16:
                    h = j - 1
                    dve.wait_ge(exp_ok, h + 1)
                    nc.vector.tensor_tensor(ee(h), ee(h), cb(h // 4), ALU.mult).then_inc(mult_ok, 1)
                if j >= 4 and j % 2 == 0:
                    c = (j - 4) // 2
                    dve.wait_ge(y_ok, 2 * c + 2)
                    y = k.pl(y0 + c)
                    nc.vector.scalar_tensor_tensor(out=y, in0=k.pl(xs + c), scalar=k.col("ssm_d", c), in1=k.bank(6 + c % 2), op0=ALU.mult, op1=ALU.add).then_inc(y_out, 1)
                    dve.wait_ge(y_out, c + 1)
                    link(nc.vector.tensor_tensor(y, y, k.pl(z + c), ALU.mult))
    return y0


def lru_phase(k, gate, xc, r, i, th):
    nc = k.nc
    pl = k.pl
    p8, m8, s0, s1, s2 = (k.small[:, 8 * n:8 * n + 8] for n in range(5))
    e_ready, e_done, p_ok = k.sem("l_e_ready"), k.sem("l_e_done"), k.sem("l_p_ok")
    a_ok, q_ok, s_ok = k.sem("l_a_ok"), k.sem("l_q_ok"), k.sem("l_s_ok")
    x_ok, h_ok = k.sem("l_x_ok"), k.sem("l_h_ok")
    with nc.Block() as block:
        @block.gpsimd
        def _(pool):
            for c in range(8):
                nc.gpsimd.tensor_tensor(pl(i + c), pl(i + c), pl(xc + c), ALU.mult).then_inc(x_ok, 1)
            for c in range(8):
                pool.wait_ge(h_ok, c + 1)
                k.pool_chain(pool, nc.gpsimd.tensor_tensor(pl(gate + c), pl(gate + c), pl(xc + c), ALU.mult))

        @block.scalar
        def _(act):
            act.wait_ge(e_ready, 1)
            nc.scalar.activation(s1, s0, ACT.Exp).then_inc(e_done, 1)
            act.wait_ge(p_ok, 1)
            for c in range(8):
                nc.scalar.activation(pl(th + c), pl(r + c), ACT.Tanh, scale=p8[:, c:c + 1]).then_inc(a_ok, 1)
                nc.scalar.activation(pl(r + c), pl(r + c), ACT.Exp, scale=m8[:, c:c + 1]).then_inc(a_ok, 1)
            for c in range(8):
                act.wait_ge(q_ok, c + 1)
                nc.scalar.activation(pl(th + c), pl(th + c), ACT.Sqrt).then_inc(s_ok, 1)

        @block.vector
        def _(dve):
            link = lambda ins: k.dve_chain(dve, ins)
            link(nc.vector.tensor_scalar(p8, k.col("lru_lam", 0, 8), -1.0, None, ALU.mult))
            softplus_steps(k, dve, None, p8, s0, s1, s2, e_done, e_ready, 0)
            link(nc.vector.tensor_scalar(m8, p8, -8.0, None, ALU.mult))
            nc.vector.tensor_scalar(p8, p8, 8.0, None, ALU.mult).then_inc(p_ok, 1)
            for c in range(8):
                dve.wait_ge(a_ok, 2 * c + 2)
                dve.wait_ge(x_ok, c + 1)
                link(nc.vector.tensor_tensor(pl(xc + c), pl(r + c), pl(r + c), ALU.mult))
                nc.vector.scalar_tensor_tensor(out=pl(th + c), in0=pl(xc + c), scalar=1.0, in1=pl(th + c), op0=ALU.add, op1=ALU.mult).then_inc(q_ok, 1)
            for c in range(8):
                dve.wait_ge(s_ok, c + 1)
                link(nc.vector.tensor_tensor(pl(i + c), pl(i + c), pl(th + c), ALU.mult))
                nc.vector.tensor_tensor_scan(pl(xc + c), pl(r + c), pl(i + c), 0.0, ALU.mult, ALU.add).then_inc(h_ok, 1)


def head_norm_steps(k, block, y, sq, rows, heads, eps, tag, finish, start=0):
    nc = k.nc
    pl = k.pl
    two = heads == 16
    width = 64 if two else P
    msum, cen, sqd, vsum, inv, root, spread, used = (k.sem(f"{tag}_{s}") for s in ("msum", "cen", "sqd", "vsum", "inv", "root", "spread", "used"))
    one, two_, per = k.const("onecol"), k.const("paircol"), heads // 8
    v, rt = rows[0:heads, :], rows[32:32 + heads, :]

    @block.tensor
    def _(pe):
        for c in range(8):
            if c >= 2:
                pe.wait_ge(cen, c - 1)
            nc.tensor.matmul(k.bank(c % 2), k.const("headsum" if two else "ones"), pl(y + c), start=True, stop=True).then_inc(msum, 1)
        for c in range(8):
            pe.wait_ge(sqd, c + 1)
            lhs = two_[:, 14 - 2 * c:30 - 2 * c] if two else one[:, 7 - c:15 - c]
            ins = nc.tensor.matmul(k.bank(2)[0:heads, :], lhs, pl(sq + c), start=(c == 0), stop=(c == 7))
        ins.then_inc(vsum, 1)
        pe.wait_ge(root, 1)
        for c in range(8):
            if c >= 2:
                pe.wait_ge(used, c - 1)
            lhs = k.const("pairsel")[0:16, c * P:(c + 1) * P] if two else k.const("sel")[0:8, c * P:(c + 1) * P]
            nc.tensor.matmul(k.bank(c % 2), lhs, v, start=True, stop=True).then_inc(spread, 1)

    @block.scalar
    def _(act):
        for c in range(8):
            act.wait_ge(cen, c + 1)
            nc.scalar.activation(pl(sq + c), pl(y + c), ACT.Square).then_inc(sqd, 1)
        act.wait_ge(inv, 1)
        nc.scalar.activation(v, v, ACT.Sqrt).then_inc(root, 1)

    @block.vector
    def _(dve):
        link = lambda ins: k.dve_chain(dve, ins)
        for c in range(8):
            dve.wait_ge(msum, c + 1)
            nc.vector.scalar_tensor_tensor(out=pl(y + c), in0=k.bank(c % 2), scalar=-1.0 / width, in1=pl(y + c), op0=ALU.mult, op1=ALU.add).then_inc(cen, 1)
        dve.wait_ge(vsum, 1)
        link(nc.vector.tensor_scalar(v, k.bank(2)[0:heads, :], 1.0 / width, eps, ALU.mult, ALU.add))
        nc.vector.reciprocal(v, v).then_inc(inv, 1)
        for c in range(8):
            dve.wait_ge(spread, c + 1)
            dve.wait_ge(cen, 8)
            nc.vector.tensor_tensor(pl(y + c), k.bank(c % 2), pl(y + c), ALU.mult).then_inc(used, 1)
            dve.wait_ge(used, c + 1)
            finish(dve, link, c)


def ret_phase(k, q, kk, v, g, y, cos, sin, table, w):
    nc = k.nc
    pl = k.pl
    rot_ok, roted = k.sem("r_rot_ok"), k.sem("r_roted")
    s_ok, d_ok, y_ok, y_out = k.sem("r_s_ok"), k.sem("r_d_ok"), k.sem("r_y_ok"), k.sem("r_y_out")
    tab = pl(table, 8).rearrange("p (h l) -> p h l", l=T)
    vt = pl(v, 8).rearrange("p (i c) -> p i c", c=D)
    ee = lambda h: pl(w, 5)[:, (h % 2) * TRI:(h % 2) * TRI + TRI]
    tmp = pl(w + 5)
    planes = [q + c for c in range(4)] + [kk + c for c in range(4)]
    with nc.Block() as block:
        @block.tensor
        def _(pe):
            for n, c in enumerate(planes):
                if n >= 2:
                    pe.wait_ge(roted, n - 1)
                nc.tensor.matmul(k.bank(n % 2), k.const("rot"), pl(c), start=True, stop=True).then_inc(rot_ok, 1)
            pe.wait_ge(roted, 8)
            for h in range(9):
                if h < 8:
                    lo = 64 * (h % 2)
                    if h >= 2:
                        pe.wait_ge(d_ok, h - 1)
                    for i in range(TT):
                        ins = nc.tensor.matmul(tri_bank(k, h % 2, i), pl(kk + h // 2)[lo:lo + 64, i * P:(i + 1) * P],
                                               pl(q + h // 2)[lo:lo + 64, i * P:T], start=True, stop=True)
                    ins.then_inc(s_ok, 1)
                if h >= 1:
                    u = h - 1
                    pe.wait_ge(d_ok, u + 1)
                    if u >= 2:
                        pe.wait_ge(y_out, u - 1)
                    for i in range(TT):
                        ins = nc.tensor.matmul(k.bank(6 + u % 2)[:, i * P:T], vt[:, i, u * P:(u + 1) * P],
                                               ee(u)[:, OFF[i]:OFF[i] + T - P * i], start=(i == 0), stop=(i == 3))
                    ins.then_inc(y_ok, 1)

        @block.vector
        def _(dve):
            link = lambda ins: k.dve_chain(dve, ins)
            for n, c in enumerate(planes):
                dve.wait_ge(rot_ok, n + 1)
                link(nc.vector.tensor_tensor(tmp, k.bank(n % 2), pl(sin), ALU.mult))
                link(nc.vector.tensor_tensor(pl(c), pl(c), pl(cos), ALU.mult))
                nc.vector.tensor_tensor(pl(c), pl(c), tmp, ALU.add).then_inc(roted, 1)
                dve.wait_ge(roted, n + 1)
            for h in range(8):
                dve.wait_ge(s_ok, h + 1)
                if h >= 2:
                    dve.wait_ge(y_ok, h - 1)
                for i in range(TT):
                    n = T - P * i
                    ins = nc.vector.scalar_tensor_tensor(out=ee(h)[:, OFF[i]:OFF[i] + n], in0=tri_bank(k, h % 2, i), scalar=0.125,
                                                         in1=tab[:, h, 0:n], op0=ALU.mult, op1=ALU.mult)
                ins.then_inc(d_ok, 1)

        @block.scalar
        def _(act):
            for h in range(8):
                act.wait_ge(y_ok, h + 1)
                nc.scalar.activation(pl(y + h), k.bank(6 + h % 2), ACT.Copy).then_inc(y_out, 1)

    def finish(dve, link, c):
        link(nc.vector.scalar_tensor_tensor(out=pl(y + c), in0=pl(y + c), scalar=k.col("ret_norm", c), in1=pl(g + c), op0=ALU.mult, op1=ALU.mult))

    with nc.Block() as block:
        head_norm_steps(k, block, y, v, pl(w + 6), 8, EPS, "rn", finish)


def rwkv_prepare_phase(k, r, kk, v, sg, a, rows, w):
    nc = k.nc
    pl = k.pl
    buf = lambda x, c: pl(w + 2 * x + c % 2)
    norm = pl(w + 10)[0:16, :]
    sq_ok, sum_ok, root, inv_ok = (k.sem(f"p_{s}") for s in ("sq_ok", "sum_ok", "root", "inv_ok"))
    cum_ok, exp_ok, spread, t4_ok, t4_used, rk_sum, c_done = (k.sem(f"p_{s}") for s in ("cum_ok", "exp_ok", "spread", "t4_ok", "t4_used", "rk_sum", "c_done"))
    with nc.Block() as block:
        @block.scalar
        def _(act):
            for c in range(8):
                if c >= 2:
                    act.wait_ge(sum_ok, c - 1)
                nc.scalar.activation(buf(4, c), pl(kk + c), ACT.Square, scale=k.col("rwkv_k_k", c)).then_inc(sq_ok, 1)
            act.wait_ge(sum_ok, 8)
            nc.scalar.activation(norm, k.bank(2)[0:16, :], ACT.Sqrt).then_inc(root, 1)
            for c in range(8):
                act.wait_ge(cum_ok, c + 1)
                if c >= 2:
                    act.wait_ge(c_done, c - 1)
                nc.scalar.activation(buf(1, c), buf(0, c), ACT.Exp).then_inc(exp_ok, 1)
                nc.scalar.activation(buf(2, c), buf(0, c), ACT.Exp, scale=-1.0).then_inc(exp_ok, 1)
                nc.scalar.activation(pl(sg + c), pl(sg + c), ACT.Exp).then_inc(exp_ok, 1)

        @block.tensor
        def _(pe):
            pair = k.const("paircol")
            for c in range(8):
                pe.wait_ge(sq_ok, c + 1)
                nc.tensor.matmul(k.bank(2)[0:16, :], pair[:, 14 - 2 * c:30 - 2 * c], buf(4, c), start=(c == 0), stop=(c == 7)).then_inc(sum_ok, 1)
            pe.wait_ge(inv_ok, 1)
            for c in range(9):
                if c < 8:
                    if c >= 2:
                        pe.wait_ge(c_done, c - 1)
                    nc.tensor.matmul(k.bank(c % 2), k.const("pairsel")[0:16, c * P:(c + 1) * P], norm, start=True, stop=True).then_inc(spread, 1)
                if c >= 1:
                    u = c - 1
                    pe.wait_ge(t4_ok, u + 1)
                    nc.tensor.matmul(k.bank(3)[0:16, :], pair[:, 14 - 2 * u:30 - 2 * u], buf(4, u), start=(u == 0), stop=(u == 7)).then_inc(t4_used, 1)

        @block.vector
        def _(dve):
            link = lambda ins: k.dve_chain(dve, ins)
            dve.wait_ge(root, 1)
            link(nc.vector.tensor_scalar(norm, norm, 1e-12, None, ALU.max))
            nc.vector.reciprocal(norm, norm).then_inc(inv_ok, 1)

            def cumulate(c):
                link(nc.vector.tensor_scalar(pl(sg + c), pl(sg + c), -float(np.exp(-0.5)), None, ALU.mult))
                if c >= 2:
                    dve.wait_ge(exp_ok, 3 * (c - 1))
                link(nc.vector.tensor_tensor_scan(buf(0, c), k.const("chunkstart"), pl(sg + c), 0.0, ALU.mult, ALU.add))
                nc.vector.tensor_tensor(pl(sg + c), buf(0, c), pl(sg + c), ALU.subtract).then_inc(cum_ok, 1)

            cumulate(0)
            for c in range(8):
                if c < 7:
                    cumulate(c + 1)
                kap, t4 = buf(3, c), buf(4, c)
                dve.wait_ge(spread, c + 1)
                link(nc.vector.scalar_tensor_tensor(out=kap, in0=pl(kk + c), scalar=k.col("rwkv_k_k", c), in1=k.bank(c % 2), op0=ALU.mult, op1=ALU.mult))
                dve.wait_ge(exp_ok, 3 * c + 3)
                link(nc.vector.tensor_copy(k.small[:, 160 + 8 * c:168 + 8 * c], buf(1, c)[:, CHUNK - 1::CHUNK]))
                link(nc.vector.tensor_tensor(pl(sg + c), pl(sg + c), kap, ALU.mult))
                link(nc.vector.tensor_tensor(kap, kap, pl(a + c), ALU.mult))
                link(nc.vector.tensor_scalar(pl(a + c), pl(a + c), -1.0, k.col("rwkv_k_a", c), ALU.add, ALU.mult))
                link(nc.vector.scalar_tensor_tensor(out=pl(kk + c), in0=pl(a + c), scalar=1.0, in1=pl(kk + c), op0=ALU.add, op1=ALU.mult))
                if c >= 2:
                    dve.wait_ge(t4_used, c - 1)
                nc.vector.scalar_tensor_tensor(out=t4, in0=pl(r + c), scalar=k.col("rwkv_r_k", c), in1=pl(kk + c), op0=ALU.mult, op1=ALU.mult).then_inc(t4_ok, 1)
                dve.wait_ge(t4_ok, c + 1)
                link(nc.vector.tensor_tensor(pl(a + c), kap, buf(2, c), ALU.mult))
                link(nc.vector.tensor_tensor(pl(kk + c), pl(kk + c), buf(2, c), ALU.mult))
                nc.vector.tensor_tensor(pl(r + c), pl(r + c), buf(1, c), ALU.mult).then_inc(c_done, 1)
                dve.wait_ge(c_done, c + 1)
            dve.wait_ge(t4_used, 8)
            link(nc.vector.tensor_copy(pl(rows)[0:16, :], k.bank(3)[0:16, :]))


def rwkv_core_phase(k, rho, kt, v, kap, bt, w):
    nc = k.nc
    pl = k.pl
    four = lambda ap: ap.rearrange("p (i t) -> p i t", i=TT)
    mask4 = lambda m: m.unsqueeze(1).broadcast_to([P, TT, P])
    at_plane = [w + n for n in range(16)] + [MRG_PL + n for n in range(8)] + [RING_PL + n for n in range(4, 12)]
    own = lambda n: pl(at_plane[n])
    XT = lambda p, h: own(11 * (p % 2) + h)
    AK = lambda p, h: own(11 * (p % 2) + 2 + h)
    AB = lambda p, h: own(11 * (p % 2) + 4 + h)
    LKV, WT, KT_, BT_, VT = (lambda p, n=n: own(11 * (p % 2) + n) for n in (6, 7, 8, 9, 10))
    LT, X, Y, LM = (lambda h, n=n: own(22 + 2 * n + h) for n in range(4))
    S = lambda n: k.pl(RING_PL)[:, (n % 4) * P:(n % 4 + 1) * P]
    NU = lambda n: k.pl(RING_PL + 1)[:, (n % 2) * P:(n % 2 + 1) * P]
    TMP = k.pl(RING_PL + 1)[:, 2 * P:3 * P]
    LKK = lambda h: pl(RING_PL + 2 + h)
    BANKS = 5
    steps = ([("tr", x, 0) for x in range(4)] + [(n, h, 0) for h in range(2) for n in ("LT", "L", "Lk", "Ak", "Ab")])
    for lev in range(1, 6):
        steps += [("Y", h, lev) for h in range(2)]
        if lev < 5:
            steps += [("X", h, lev) for h in range(2)]
        steps += [("XT", h, lev) for h in range(2)]
    steps += [("LkV", 0, 0), ("WT", 0, 0)]
    N = len(steps)
    by_act = [s[0] in ("tr", "Y", "LkV", "WT") for s in steps]
    nact, ndve = sum(by_act), N - sum(by_act)

    def at(p, *s):
        return p * N + steps.index(s) + 1

    def emptied(g):
        p, n = divmod(g, N)
        if by_act[n]:
            return act_out, p * nact + sum(by_act[:n + 1])
        return dve_out, p * ndve + (n + 1 - sum(by_act[:n + 1]))

    made, act_out, dve_out, lm_ok = k.sem("w_made"), k.sem("w_act_out"), k.sem("w_dve_out"), k.sem("w_lm_ok")
    u_ok, nu_ok, ds_ok, st_ok, o_ok, o_out = (k.sem(f"w_{s}") for s in ("u_ok", "nu_ok", "ds_ok", "st_ok", "o_ok", "o_out"))

    def slices(n):
        return range(n * N // 16, (n + 1) * N // 16)

    with nc.Block() as block:
        @block.tensor
        def _(pe):
            def make(p, n):
                kind, h, lev = steps[n]
                g = p * N + n
                if g >= BANKS:
                    pe.wait_ge(*emptied(g - BANKS))
                out = k.bank(g % BANKS)
                rows = slice(64 * h, 64 * h + 64)
                if kind in ("Y", "X", "XT"):
                    if kind == "Y":
                        pe.wait_ge(lm_ok, 10 * p + 2 * (lev - 1) + h + 1)
                        if lev == 1:
                            pe.wait_ge(*emptied(at(p, "L", h, 0) - 1))
                        else:
                            pe.wait_ge(*emptied(at(p, "X", h, lev - 1) - 1))
                    else:
                        pe.wait_ge(*emptied(at(p, "Y", h, lev) - 1))
                        if lev == 1:
                            pe.wait_ge(*emptied(at(p, "LT", h, 0) - 1))
                        else:
                            pe.wait_ge(*emptied(at(p, "XT", h, lev - 1) - 1))
                if kind in ("LkV", "WT"):
                    for hh in range(2):
                        if kind == "LkV":
                            pe.wait_ge(*emptied(at(p, "Lk", hh, 0) - 1))
                            pe.wait_ge(*emptied(at(p, "tr", 3, 0) - 1))
                        else:
                            pe.wait_ge(*emptied(at(p, "XT", hh, 5) - 1))
                            pe.wait_ge(*emptied(at(p, "tr", 0, 0) - 1))
                for i in range(TT):
                    t = slice(i * P, (i + 1) * P)
                    mm = lambda l, r: nc.tensor.matmul(out[:, t], l, r, start=True, stop=True)
                    if kind == "tr":
                        ins = nc.tensor.transpose(out[:, t], pl((kap, kt, bt, v)[h] + p)[:, t], k.const("ident"))
                    elif kind == "LT":
                        ins = mm(pl(bt + p)[rows, t], pl(kap + p)[rows, t])
                    elif kind == "L":
                        ins = mm(pl(kap + p)[rows, t], pl(bt + p)[rows, t])
                    elif kind == "Lk":
                        ins = mm(pl(kt + p)[rows, t], pl(kap + p)[rows, t])
                    elif kind == "Ak":
                        ins = mm(pl(kt + p)[rows, t], pl(rho + p)[rows, t])
                    elif kind == "Ab":
                        ins = mm(pl(bt + p)[rows, t], pl(rho + p)[rows, t])
                    elif kind == "Y":
                        ins = mm(LM(h)[:, t], X(h)[:, t])
                    elif kind == "X":
                        ins = mm(XT(p, h)[:, t], Y(h)[:, t])
                    elif kind == "XT":
                        ins = mm(Y(h)[:, t], XT(p, h)[:, t])
                    elif kind == "LkV":
                        for hh in range(2):
                            c = slice(i * P + 64 * hh, i * P + 64 * hh + 64)
                            ins = nc.tensor.matmul(out[:, c], LKK(hh)[:, t], VT(p)[:, c], start=True, stop=True)
                    elif kind == "WT":
                        for hh in range(2):
                            ins = nc.tensor.matmul(out[64 * hh:64 * hh + 64, t], WT(p)[:, i * P + 64 * hh:i * P + 64 * hh + 64],
                                                   XT(p, hh)[:, t], start=True, stop=True)
                ins.then_inc(made, 1)

            def chunk_u(p, j):
                i, lo = j // 2, 64 * (j % 2)
                n = 8 * p + j
                t = slice(i * P + lo, i * P + lo + 64)
                pe.wait_ge(*emptied(at(p, "WT", 0, 0) - 1))
                pe.wait_ge(*emptied(at(p, "LkV", 0, 0) - 1))
                pe.wait_ge(st_ok, n + 1)
                if n >= 1:
                    pe.wait_ge(nu_ok, n)
                u = k.bank(5)[lo:lo + 64, 0:P]
                nc.tensor.matmul(u, WT(p)[:, t], S(n), start=True, stop=False, skip_group_check=True)
                for h in range(2):
                    ins = nc.tensor.matmul(u[:, 64 * h:64 * h + 64], XT(p, h)[:, t], LKV(p)[:, i * P + 64 * h:i * P + 64 * h + 64],
                                           start=False, stop=True, skip_group_check=True)
                ins.then_inc(u_ok, 1)

            def chunk_state(p, j):
                i, lo = j // 2, 64 * (j % 2)
                n = 8 * p + j
                pe.wait_ge(nu_ok, n + 1)
                rows = slice(lo, lo + 64)
                nc.tensor.matmul(k.bank(6)[:, 0:P], KT_(p)[rows, i * P:(i + 1) * P], VT(p)[rows, i * P:(i + 1) * P], start=True, stop=False)
                nc.tensor.matmul(k.bank(6)[:, 0:P], BT_(p)[rows, i * P:(i + 1) * P], NU(n // 2)[rows, :], start=False, stop=True).then_inc(ds_ok, 1)
                if j % 2 == 1:
                    m = n // 2
                    if m >= 1:
                        pe.wait_ge(o_out, m)
                    o = k.bank(7)[:, 0:P]
                    for q in range(2):
                        nc.tensor.matmul(o[:, 64 * q:64 * q + 64], S(n - 1 + q), pl(rho + p)[:, i * P + 64 * q:i * P + 64 * q + 64],
                                         start=(q == 0), stop=False, skip_group_check=True)
                    for h in range(2):
                        c = slice(64 * h, 64 * h + 64)
                        nc.tensor.matmul(o[c, :], VT(p)[:, i * P + 64 * h:i * P + 64 * h + 64], AK(p, h)[:, i * P:(i + 1) * P],
                                         start=False, stop=False, skip_group_check=True)
                        ins = nc.tensor.matmul(o[c, :], NU(m)[:, c], AB(p, h)[:, i * P:(i + 1) * P],
                                               start=False, stop=True, skip_group_check=True)
                    ins.then_inc(o_ok, 1)

            for p in range(9):
                for j in range(8):
                    for part in range(2):
                        if p < 8:
                            for n in slices(2 * j + part):
                                make(p, n)
                        if p >= 1:
                            (chunk_u, chunk_state)[part](p - 1, j)

        @block.scalar
        def _(act):
            def make(p, n):
                kind, h, lev = steps[n]
                g = p * N + n
                act.wait_ge(made, g + 1)
                dst = {"tr": lambda: (WT, KT_, BT_, VT)[h](p), "Y": lambda: Y(h), "LkV": lambda: LKV(p), "WT": lambda: WT(p)}[kind]()
                nc.scalar.activation(dst, k.bank(g % BANKS), ACT.Copy).then_inc(act_out, 1)

            for p in range(9):
                for j, part in [(j, part) for j in range(8) for part in range(2)]:
                    if p < 8:
                        for n in slices(2 * j + part):
                            if by_act[n]:
                                make(p, n)
                    if p >= 1:
                        n = 8 * (p - 1) + j
                        lo = 64 * (j % 2)
                        if part == 0:
                            act.wait_ge(u_ok, n + 1)
                            nc.scalar.activation(NU(n // 2)[lo:lo + 64, :], k.bank(5)[lo:lo + 64, 0:P], ACT.Copy, scale=-1.0).then_inc(nu_ok, 1)
                        elif j % 2 == 1:
                            act.wait_ge(o_ok, n // 2 + 1)
                            nc.scalar.activation(pl(rho + p - 1)[:, (j // 2) * P:(j // 2 + 1) * P], k.bank(7)[:, 0:P], ACT.Copy).then_inc(o_out, 1)

        @block.gpsimd
        def _(pool):
            for p in range(8):
                for lev in range(1, 6):
                    for h in range(2):
                        if lev == 1:
                            pool.wait_ge(*emptied(at(p, "LT", h, 0) - 1))
                            if p >= 1:
                                pool.wait_ge(made, at(p - 1, "Y", h, 5))
                        else:
                            pool.wait_ge(made, at(p, "Y", h, lev - 1))
                        nc.gpsimd.tensor_tensor(four(LM(h)), four(LT(h)), mask4(k.const("level")[:, lev * P:(lev + 1) * P]), ALU.mult).then_inc(lm_ok, 1)

        @block.vector
        def _(dve):
            link = lambda ins: k.dve_chain(dve, ins)

            def make(p, n):
                kind, h, lev = steps[n]
                g = p * N + n
                dve.wait_ge(made, g + 1)
                ps = four(k.bank(g % BANKS))
                m = lambda dst, name: nc.vector.tensor_tensor(four(dst), ps, mask4(k.const(name)), ALU.mult)
                if kind == "LT":
                    if p >= 1:
                        dve.wait_ge(lm_ok, 10 * p)
                    level0 = k.const("level")[:, 0:P]
                    link(nc.vector.scalar_tensor_tensor(out=four(XT(p, h)), in0=ps, scalar=-1.0, in1=mask4(level0), op0=ALU.mult, op1=ALU.mult))
                    link(nc.vector.tensor_tensor(four(XT(p, h)), four(XT(p, h)), mask4(k.const("ident")), ALU.add))
                    ins = m(LT(h), "strict")
                elif kind == "L":
                    link(nc.vector.scalar_tensor_tensor(out=four(X(h)), in0=ps, scalar=-1.0, in1=mask4(k.const("levelT")[:, 0:P]), op0=ALU.mult, op1=ALU.mult))
                    ins = nc.vector.tensor_tensor(four(X(h)), four(X(h)), mask4(k.const("ident")), ALU.add)
                elif kind == "Lk":
                    ins = m(LKK(h), "strict")
                elif kind == "Ak":
                    ins = m(AK(p, h), "incl")
                elif kind == "Ab":
                    ins = m(AB(p, h), "incl")
                elif kind == "X":
                    ins = nc.vector.tensor_tensor(X(h), X(h), k.bank(g % BANKS), ALU.subtract)
                elif kind == "XT":
                    ins = nc.vector.tensor_tensor(XT(p, h), XT(p, h), k.bank(g % BANKS), ALU.subtract)
                ins.then_inc(dve_out, 1)

            for p in range(9):
                if p >= 1:
                    nc.vector.memset(S(8 * (p - 1)), 0.0).then_inc(st_ok, 1)
                for j in range(8):
                    if p < 8:
                        for n in [*slices(2 * j), *slices(2 * j + 1)]:
                            if not by_act[n]:
                                make(p, n)
                    if p >= 1 and j < 7:
                        n = 8 * (p - 1) + j
                        ec = k.small[:, 160 + n:161 + n]
                        dve.wait_ge(ds_ok, n + 1)
                        dve.wait_ge(st_ok, n + 1)
                        link(nc.vector.scalar_tensor_tensor(out=TMP, in0=k.bank(6)[:, 0:P], scalar=ec, in1=k.const("headsum"), op0=ALU.mult, op1=ALU.mult))
                        nc.vector.scalar_tensor_tensor(out=S(n + 1), in0=S(n), scalar=ec, in1=TMP, op0=ALU.mult, op1=ALU.add).then_inc(st_ok, 1)


def rwkv_finish_phase(k, y, v, rows, w):
    nc = k.nc
    pl = k.pl

    def finish(dve, link, c):
        link(nc.vector.tensor_scalar(pl(y + c), pl(y + c), k.col("rwkv_ln_w", c), k.col("rwkv_ln_b", c), ALU.mult, ALU.add))

    with nc.Block() as block:
        head_norm_steps(k, block, y, w, pl(w + 8), 16, 64e-5, "wn", finish)
    spread, used = k.sem("f_spread"), k.sem("f_used")
    with nc.Block() as block:
        @block.tensor
        def _(pe):
            for c in range(8):
                if c >= 2:
                    pe.wait_ge(used, c - 1)
                nc.tensor.matmul(k.bank(c % 2), k.const("pairsel")[0:16, c * P:(c + 1) * P], pl(rows)[0:16, :], start=True, stop=True).then_inc(spread, 1)

        @block.vector
        def _(dve):
            for c in range(8):
                dve.wait_ge(spread, c + 1)
                nc.vector.tensor_tensor(pl(v + c), k.bank(c % 2), pl(v + c), ALU.mult).then_inc(used, 1)
                dve.wait_ge(used, c + 1)
                k.dve_chain(dve, nc.vector.tensor_tensor(pl(y + c), pl(y + c), pl(v + c), ALU.add))


def columns_phase(k, steps):
    with k.nc.Block() as block:
        @block.vector
        def _(dve):
            for step in steps:
                k.dve_chain(dve, step())


def l2_rope_phase(k, tag, planes, n, w, cos=None, sin=None, mean=1.0, finish=None):
    nc = k.nc
    pl = k.pl
    m = len(planes)
    sqd, vsum, inv, root, spread, used, turned, done = (k.sem(f"{tag}_{s}") for s in ("sqd", "vsum", "inv", "root", "spread", "used", "turned", "done"))
    sq = lambda c: pl(w + c)[:, 0:n]
    rows, tmp = pl(w + 8)[0:m, 0:n], pl(w + 9)[:, 0:n]
    one = k.const("onecol")
    with nc.Block() as block:
        @block.scalar
        def _(act):
            for c in range(m):
                nc.scalar.activation(sq(c), planes[c], ACT.Square).then_inc(sqd, 1)
            act.wait_ge(inv, 1)
            nc.scalar.activation(rows, rows, ACT.Sqrt).then_inc(root, 1)

        @block.tensor
        def _(pe):
            for c in range(m):
                pe.wait_ge(sqd, c + 1)
                ins = nc.tensor.matmul(k.bank(2)[0:m, 0:n], one[:, 7 - c:7 - c + m], sq(c), start=(c == 0), stop=(c == m - 1))
            ins.then_inc(vsum, 1)
            pe.wait_ge(root, 1)
            for c in range(m):
                if c >= 2:
                    pe.wait_ge(used, c - 1)
                nc.tensor.matmul(k.bank(c % 2)[:, 0:n], k.const("sel")[0:m, c * P:(c + 1) * P], rows, start=True, stop=True).then_inc(spread, 1)
            if cos is not None:
                for c in range(m):
                    pe.wait_ge(used, c + 1)
                    if c >= 2:
                        pe.wait_ge(done, c - 1)
                    nc.tensor.matmul(k.bank(3 + c % 2)[:, 0:n], k.const("rot"), planes[c], start=True, stop=True).then_inc(turned, 1)

        @block.vector
        def _(dve):
            link = lambda ins: k.dve_chain(dve, ins)
            dve.wait_ge(vsum, 1)
            link(nc.vector.tensor_scalar(rows, k.bank(2)[0:m, 0:n], mean, EPS, ALU.mult, ALU.add))
            nc.vector.reciprocal(rows, rows).then_inc(inv, 1)
            for c in range(m):
                dve.wait_ge(spread, c + 1)
                nc.vector.tensor_tensor(planes[c], k.bank(c % 2)[:, 0:n], planes[c], ALU.mult).then_inc(used, 1)
                if finish is not None:
                    dve.wait_ge(used, c + 1)
                    link(finish(c))
            if cos is not None:
                for c in range(m):
                    dve.wait_ge(turned, c + 1)
                    link(nc.vector.tensor_tensor(tmp, k.bank(3 + c % 2)[:, 0:n], sin, ALU.mult))
                    link(nc.vector.tensor_tensor(planes[c], planes[c], cos, ALU.mult))
                    nc.vector.tensor_tensor(planes[c], planes[c], tmp, ALU.add).then_inc(done, 1)
                    dve.wait_ge(done, c + 1)


def attention_phase(k, q, kt, v, kc, vc, y, w):
    nc = k.nc
    pl = k.pl
    NK = T + CTX
    units = [(h, i) for h in range(8) for i in range(TT)]
    B = lambda n: pl(w + n % 3)
    Sx = lambda n: pl(w + 3, 5)[:, (n % 3) * NK:(n % 3) * NK + NK]
    PT = lambda n: pl(w + 8, 3)[:, (n % 2) * NK:(n % 2) * NK + NK]
    cols = k.small
    b_in = [k.sem(f"a_b_in{i}") for i in range(3)]
    s_ok, s_used, max_ok, e_ok, p_ok, t_ok, t_out, y_ok, y_out = (k.sem(f"a_{s}") for s in ("s_ok", "s_used", "max_ok", "e_ok", "p_ok", "t_ok", "t_out", "y_ok", "y_out"))
    with nc.Block() as block:
        @block.sync
        def _(sp):
            for n, (h, i) in enumerate(units):
                if n >= 3:
                    sp.wait_ge(s_used, n - 2)
                for r in range(2):
                    row = 2 * i + r
                    sp.dma_start(B(n)[64 * r:64 * r + 64, :], k.dram["rpb"][h, :, (7 - row) * 64:(15 - row) * 64]).then_inc(b_in[n % 3], 16)

        @block.tensor
        def _(pe):
            def scores(n):
                h, i = units[n]
                lo = 64 * (h % 2)
                if n >= 2:
                    pe.wait_ge(s_used, n - 1)
                a, b = k.bank(2 * (n % 2)), k.bank(2 * (n % 2) + 1)[:, 0:CTX]
                lhs = pl(q + h // 2)[lo:lo + 64, i * P:(i + 1) * P]
                nc.tensor.matmul(a, lhs, pl(kt + h // 2)[lo:lo + 64, :], start=True, stop=True)
                nc.tensor.matmul(b, lhs, kc[lo:lo + 64, h // 2, :], start=True, stop=True).then_inc(s_ok, 1)

            def values(n):
                h, i = units[n]
                lo = 64 * (h % 2)
                pe.wait_ge(t_out, n + 1)
                if n >= 2:
                    pe.wait_ge(y_out, n - 1)
                out = k.bank(6 + n % 2)[lo:lo + 64, 0:P]
                for j in range(6):
                    vv = v[:, j, h * 64:h * 64 + 64] if j < 4 else vc[:, j - 4, h * 64:h * 64 + 64]
                    ins = nc.tensor.matmul(out, vv, PT(n)[:, j * P:(j + 1) * P], start=(j == 0), stop=(j == 5))
                ins.then_inc(y_ok, 1)

            scores(0)
            scores(1)
            for n in range(len(units) + 1):
                if n + 2 < len(units):
                    scores(n + 2)
                if n >= 1:
                    values(n - 1)
                if n < len(units):
                    pe.wait_ge(p_ok, n + 1)
                    if n >= 1:
                        pe.wait_ge(t_out, n)
                    for j in range(6):
                        ins = nc.tensor.transpose(k.bank(4 + j // 4)[:, (j % 4) * P:(j % 4 + 1) * P], Sx(n)[:, j * P:(j + 1) * P], k.const("ident"))
                    ins.then_inc(t_ok, 1)

        @block.vector
        def _(dve):
            link = lambda ins: k.dve_chain(dve, ins)

            def logits(n):
                dve.wait_ge(s_ok, n + 1)
                dve.wait_ge(b_in[n % 3], 32 * (n // 3 + 1))
                if n >= 3:
                    dve.wait_ge(t_ok, n - 2)
                nc.vector.tensor_scalar(Sx(n)[:, T:NK], k.bank(2 * (n % 2) + 1)[:, 0:CTX], 0.125, None, ALU.mult)
                nc.vector.scalar_tensor_tensor(out=Sx(n)[:, 0:T], in0=k.bank(2 * (n % 2)), scalar=0.125, in1=B(n), op0=ALU.mult, op1=ALU.add).then_inc(s_used, 1)
                dve.wait_ge(s_used, n + 1)
                link(nc.vector.tensor_reduce(cols[:, 2 * (n % 3):2 * (n % 3) + 1], Sx(n), AX.X, ALU.max))
                nc.vector.tensor_scalar(cols[:, 2 * (n % 3):2 * (n % 3) + 1], cols[:, 2 * (n % 3):2 * (n % 3) + 1], -1.0, None, ALU.mult).then_inc(max_ok, 1)

            logits(0)
            logits(1)
            for n in range(len(units)):
                dve.wait_ge(e_ok, n + 1)
                s = cols[:, 2 * (n % 3) + 1:2 * (n % 3) + 2]
                link(nc.vector.reciprocal(s, s))
                nc.vector.tensor_scalar(Sx(n), Sx(n), s, None, ALU.mult).then_inc(p_ok, 1)
                if n + 2 < len(units):
                    logits(n + 2)

        def store(act, n):
            h, i = units[n]
            lo = 64 * (h % 2)
            act.wait_ge(y_ok, n + 1)
            nc.scalar.activation(pl(y + h // 2)[lo:lo + 64, i * P:(i + 1) * P], k.bank(6 + n % 2)[lo:lo + 64, 0:P], ACT.Copy).then_inc(y_out, 1)

        @block.scalar
        def _(act):
            def exps(n):
                act.wait_ge(max_ok, n + 1)
                c = 2 * (n % 3)
                nc.scalar.activation(Sx(n), Sx(n), ACT.Exp, bias=cols[:, c:c + 1], accum_out=cols[:, c + 1:c + 2]).then_inc(e_ok, 1)

            exps(0)
            exps(1)
            for n in range(len(units)):
                act.wait_ge(t_ok, n + 1)
                if n >= 2:
                    act.wait_ge(y_ok, n - 1)
                nc.scalar.activation(PT(n)[:, 0:512], k.bank(4), ACT.Copy)
                nc.scalar.activation(PT(n)[:, 512:768], k.bank(5)[:, 0:256], ACT.Copy).then_inc(t_out, 1)
                if n >= 1:
                    store(act, n - 1)
                if n + 2 < len(units):
                    exps(n + 2)
            store(act, len(units) - 1)


def gdn_slot(g, s):
    return (True, 2 * g + s // 2, s % 2) if g < 2 else (False, g - 2, s)


def gdn_col(d, g):
    return 32 + 8 * d + 4 * g if g < 2 else 16 * d + 4 * (g - 2)


C_G, C_BETA, C_GC, C_EGC, C_KD, C_END, C_BE = 0, 48, 96, 144, 192, 240, 336


def gdn_columns_phase(k, ab, cp, sp0):
    nc = k.nc
    col = k.pl(cp)
    arr = lambda c, n=48: col[:, c:c + n]
    g, beta, gc = arr(C_G), arr(C_BETA), arr(C_GC)
    s = [k.pl(sp0)[:, 48 * n:48 * n + 48] for n in range(3)]
    na, back = k.pl(sp0)[:, 144:152], k.pl(sp0)[:, 160:208]
    rows, sums16 = k.pl(sp0 + 1)[0:48, 0:256], k.pl(sp0 + 1)[0:48, 256:272]
    ends = k.pl(sp0 + 2)
    in_ok, sig, e_ready, e_done, g_ok = (k.sem(f"c_{x}") for x in ("in_ok", "sig", "e_ready", "e_done", "g_ok"))
    rows_in, rows_ok, cols_ok, back_ok, flip_ok, gc_ok, end_in, end_ok, exps = (k.sem(f"c_{x}") for x in ("rows_in", "rows_ok", "cols_ok", "back_ok", "flip_ok", "gc_ok", "end_in", "end_ok", "exps"))
    by = lambda x, n: (x[:, 0:32].rearrange("p (m i) -> p m i", i=4), x[:, 32:48].rearrange("p (m i) -> p m i", i=2))[n]
    FORWARD, BACKWARD = ((0, 16), (32, 40)), ((16, 32), (40, 48))
    with nc.Block() as block:
        @block.scalar
        def _(act):
            act.wait_ge(in_ok, 1)
            nc.scalar.activation(beta, beta, ACT.Sigmoid).then_inc(sig, 1)
            nc.scalar.activation(na, k.col("gdn_a_log", 0, 8), ACT.Exp).then_inc(sig, 1)
            act.wait_ge(e_ready, 1)
            nc.scalar.activation(s[1], s[0], ACT.Exp).then_inc(e_done, 1)
            act.wait_ge(end_ok, 1)
            nc.scalar.activation(arr(C_EGC), gc, ACT.Exp).then_inc(exps, 1)
            nc.scalar.activation(arr(C_KD, 144), arr(C_KD, 144), ACT.Exp).then_inc(exps, 1)

        @block.tensor
        def _(pe):
            ident, flip = k.const("ident"), k.const("flip")
            pe.wait_ge(g_ok, 1)
            nc.tensor.matmul(k.bank(0)[0:48, 0:P], g, ident, start=True, stop=True)
            nc.tensor.matmul(k.bank(0)[0:48, P:2 * P], g, flip, start=True, stop=True).then_inc(rows_in, 1)
            pe.wait_ge(rows_ok, 1)
            for n in range(2):
                ins = nc.tensor.transpose(k.bank(1)[:, 48 * n:48 * n + 48], rows[:, n * P:(n + 1) * P], ident[0:48, 0:48])
            ins.then_inc(cols_ok, 1)
            pe.wait_ge(back_ok, 1)
            nc.tensor.matmul(k.bank(2)[:, 0:48], flip, back, start=True, stop=True).then_inc(flip_ok, 1)
            pe.wait_ge(gc_ok, 1)
            for n in range(4):
                ins = nc.tensor.matmul(k.bank(3)[:, 48 * n:48 * n + 48], ends[:, n * P:(n + 1) * P], gc, start=True, stop=True)
            ins.then_inc(end_in, 1)

        @block.vector
        def _(dve):
            link = lambda ins: k.dve_chain(dve, ins)
            for n, (lo, hi) in enumerate(((0, 4), (4, 6))):
                bias = k.col("gdn_dt_bias", 0, 8).unsqueeze(2).broadcast_to([P, 8, hi - lo])
                link(nc.vector.tensor_tensor(by(g, n), ab[:, lo:hi, 0:8].rearrange("p i m -> p m i"), bias, ALU.add))
                link(nc.vector.tensor_copy(by(beta, n), ab[:, lo:hi, 8:16].rearrange("p i m -> p m i")))
            nc.vector.engine_nop().then_inc(in_ok, 1)
            for n, t in enumerate((63, 127, 0, 64)):
                link(nc.vector.tensor_scalar(ends[:, n * P:(n + 1) * P], k.const("ones"), k.const("ident")[:, t:t + 1], None, ALU.mult))
            softplus_steps(k, dve, None, g, s[0], s[1], s[2], e_done, e_ready, 0)
            dve.wait_ge(sig, 2)
            link(nc.vector.tensor_scalar(na, na, -1.0, None, ALU.mult))
            for n, w in enumerate((4, 2)):
                link(nc.vector.tensor_tensor(by(g, n), by(g, n), na.unsqueeze(2).broadcast_to([P, 8, w]), ALU.mult))
            nc.vector.engine_nop().then_inc(g_ok, 1)
            dve.wait_ge(rows_in, 1)
            for n in range(2):
                link(nc.vector.tensor_tensor_scan(rows[:, n * P:(n + 1) * P], k.const("every16")[0:48, :], k.bank(0)[0:48, n * P:(n + 1) * P], 0.0, ALU.mult, ALU.add))
            link(nc.vector.tensor_tensor_scan(sums16, k.const("chunkstart")[0:48, 0:256:16], rows[:, 15::16], 0.0, ALU.mult, ALU.add))
            late = rows.rearrange("p (q b t) -> p q b t", b=4, t=16)[:, :, 1:4, :]
            before = sums16.rearrange("p (q b) -> p q b", b=4)[:, :, 0:3].unsqueeze(3).broadcast_to([48, 4, 3, 16])
            nc.vector.tensor_tensor(late, late, before, ALU.add).then_inc(rows_ok, 1)
            dve.wait_ge(cols_ok, 1)
            nc.vector.tensor_copy(back, k.bank(1)[:, 48:96]).then_inc(back_ok, 1)
            for lo, hi in FORWARD:
                link(nc.vector.tensor_copy(gc[:, lo:hi], k.bank(1)[:, lo:hi]))
            dve.wait_ge(flip_ok, 1)
            for lo, hi in BACKWARD:
                link(nc.vector.tensor_copy(gc[:, lo:hi], k.bank(2)[:, lo:hi]))
            nc.vector.engine_nop().then_inc(gc_ok, 1)
            dve.wait_ge(end_in, 1)
            for half in range(2):
                for cols, n in ((FORWARD, half), (BACKWARD, 2 + half)):
                    for lo, hi in cols:
                        link(nc.vector.tensor_copy(arr(C_END + 48 * half)[:, lo:hi], k.bank(3)[:, 48 * n + lo:48 * n + hi]))
                rows_ = slice(64 * half, 64 * half + 64)
                link(nc.vector.tensor_tensor(arr(C_KD)[rows_, :], arr(C_END + 48 * half)[rows_, :], gc[rows_, :], ALU.subtract))
            nc.vector.engine_nop().then_inc(end_ok, 1)
            dve.wait_ge(exps, 2)
            link(nc.vector.tensor_tensor(arr(C_BE), beta, arr(C_EGC), ALU.mult))


def gdn_make_phase(k, d, qs, ks, vs, cp, keep, own):
    nc = k.nc
    four = lambda ap: ap.rearrange("p (i t) -> p i t", i=TT)
    mask4 = lambda m: m.unsqueeze(1).broadcast_to([P, TT, P])
    col = k.pl(cp)
    c4 = lambda base, g: col[:, base + gdn_col(d, g):base + gdn_col(d, g) + 4].unsqueeze(2).broadcast_to([P, TT, P])
    inc = k.const(("incl", "inclT")[d])
    after = k.const(("strictT", "strict")[d])
    level, levelT = k.const(("level", "levelT")[d]), k.const(("levelT", "level")[d])[:, 0:P]
    LT, X, XT, Y, LM, DD, KP, BV = (lambda h, n=n: k.pl(own[2 * n + h]) for n in range(8))
    SCALE = float(128 ** -0.5)
    BANKS = 8
    steps = []
    for p in range(3):
        lat = p > 0
        st = []
        for kind in ("R", "kt", "vt", "KK", "LT") + (("AT",) if lat else ()):
            st += [(p, kind, h, 0) for h in range(2)]
        for lev in range(1, 6):
            for kind in ("Y", "XT", "X") if lev < 5 else ("Y", "XT"):
                st += [(p, kind, h, lev) for h in range(2)]
        st += [(p, kind, h, 0) for kind in ("U0", "W") for h in range(2)]
        steps += st
    on_act = [s[1] in ("X", "Y", "U0", "W") for s in steps]
    made, act_out, dve_out, pre_ok, lm_ok, mask_ok, exp_ok = (k.sem(f"g{d}_{x}") for x in ("made", "act_out", "dve_out", "pre_ok", "lm_ok", "mask_ok", "exp_ok"))

    def emptied(n):
        a = sum(on_act[:n + 1])
        return (act_out, a) if on_act[n] else (dve_out, n + 1 - a)

    at = lambda *s: steps.index(s)

    def exps_before(p, h):
        return (0, 4, 10)[p] + h * (3 if p else 2)

    with nc.Block() as block:
        @block.tensor
        def _(pe):
            for n, (p, kind, h, lev) in enumerate(steps):
                g = 2 * p + h
                if n >= BANKS:
                    pe.wait_ge(*emptied(n - BANKS))
                if kind == "R":
                    pe.wait_ge(pre_ok, g + 1)
                elif kind == "LT":
                    pe.wait_ge(*emptied(at(p, "KK", h, 0)))
                elif kind == "Y":
                    pe.wait_ge(lm_ok, 10 * p + 2 * (lev - 1) + h + 1)
                    pe.wait_ge(*emptied(at(p, "LT", h, 0) if lev == 1 else at(p, "X", h, lev - 1)))
                elif kind == "X":
                    pe.wait_ge(*emptied(at(p, "XT", h, lev)))
                elif kind == "XT":
                    pe.wait_ge(*emptied(at(p, "Y", h, lev)))
                    pe.wait_ge(*emptied(at(p, "LT", h, 0) if lev == 1 else at(p, "XT", h, lev - 1)))
                elif kind in ("U0", "W"):
                    pe.wait_ge(*emptied(at(p, "XT", h, 5)))
                    pe.wait_ge(*emptied(at(p, "kt", h, 0)))
                    pe.wait_ge(*emptied(at(p, "vt", h, 0)))
                for s in range(TT):
                    ctx, head, tile = gdn_slot(g, s)
                    t, o = slice(s * P, (s + 1) * P), slice(tile * P, (tile + 1) * P)
                    out = k.bank(n % BANKS)[:, t]
                    mm = lambda l, r: nc.tensor.matmul(out, l, r, start=True, stop=True)
                    kh, vh = ks(ctx, head)[:, o], vs(ctx, head)[:, o]
                    if kind == "R":
                        ins = mm(LM(h)[:, t], k.const("ident"))
                    elif kind == "kt":
                        ins = nc.tensor.transpose(out, kh, k.const("ident"))
                    elif kind == "vt":
                        ins = nc.tensor.transpose(out, vh, k.const("ident"))
                    elif kind == "KK":
                        ins = mm(kh, kh)
                    elif kind == "LT":
                        ins = nc.tensor.transpose(out, X(h)[:, t], k.const("ident"))
                    elif kind == "AT":
                        ins = mm(kh, qs(head)[:, o])
                    elif kind == "Y":
                        ins = mm(LM(h)[:, t], X(h)[:, t])
                    elif kind == "X":
                        ins = nc.tensor.transpose(out, XT(h)[:, t], k.const("ident"))
                    elif kind == "XT":
                        ins = mm(Y(h)[:, t], XT(h)[:, t])
                    elif kind == "U0":
                        ins = mm(XT(h)[:, t], BV(h)[:, t])
                    elif kind == "W":
                        ins = mm(KP(h)[:, t], XT(h)[:, t])
                ins.then_inc(made, 1)

        @block.scalar
        def _(act):
            for n, (p, kind, h, lev) in enumerate(steps):
                g = 2 * p + h
                if kind == "R":
                    act.wait_ge(*emptied(n))
                    nc.scalar.activation(DD(h), DD(h), ACT.Exp).then_inc(exp_ok, 1)
                    nc.scalar.activation(XT(h), XT(h), ACT.Exp, scale=-1.0).then_inc(exp_ok, 1)
                    if p:
                        nc.scalar.activation(keep(g, "QD"), keep(g, "QD"), ACT.Exp).then_inc(exp_ok, 1)
                if not on_act[n]:
                    continue
                act.wait_ge(made, n + 1)
                dst = {"X": X(h), "Y": Y(h), "U0": keep(g, "U0"), "W": keep(g, "W")}[kind]
                nc.scalar.activation(dst, k.bank(n % BANKS), ACT.Copy).then_inc(act_out, 1)

        @block.gpsimd
        def _(pool):
            for p in range(3):
                for h in range(2):
                    for e, x, m in ((1, DD(h), inc), (2, XT(h), after)):
                        pool.wait_ge(exp_ok, exps_before(p, h) + e)
                        nc.gpsimd.tensor_tensor(four(x), four(x), mask4(m), ALU.mult).then_inc(mask_ok, 1)
                for lev in range(1, 6):
                    for h in range(2):
                        if lev == 1:
                            pool.wait_ge(*emptied(at(p, "LT", h, 0)))
                        else:
                            pool.wait_ge(made, at(p, "Y", h, lev - 1) + 1)
                        nc.gpsimd.tensor_tensor(four(LM(h)), four(LT(h)), mask4(level[:, lev * P:(lev + 1) * P]), ALU.mult).then_inc(lm_ok, 1)

        @block.vector
        def _(dve):
            link = lambda ins: k.dve_chain(dve, ins)

            def pre(p):
                for h in range(2):
                    g = 2 * p + h
                    nc.vector.tensor_tensor(four(LM(h)), mask4(k.const("ones")), c4(C_GC, g), ALU.mult).then_inc(pre_ok, 1)

            for n, (p, kind, h, lev) in enumerate(steps):
                g = 2 * p + h
                if kind == "R" and h == 0:
                    pre(p)
                if on_act[n]:
                    continue
                dve.wait_ge(made, n + 1)
                ps = four(k.bank(n % BANKS))
                tt = lambda o, a, b, op=ALU.mult: nc.vector.tensor_tensor(o, a, b, op)
                if kind == "R":
                    if p:
                        link(nc.vector.tensor_copy(keep(g, "QD"), k.bank(n % BANKS)))
                    link(tt(four(DD(h)), ps, c4(C_GC, g), ALU.subtract))
                    link(nc.vector.tensor_scalar(XT(h), DD(h), 0.0, None, ALU.max))
                    ins = nc.vector.tensor_scalar(DD(h), DD(h), 0.0, None, ALU.min)
                elif kind == "kt":
                    link(tt(four(KP(h)), ps, c4(C_BE, g)))
                    ins = tt(four(keep(g, "KD")), ps, c4(C_KD, g))
                elif kind == "vt":
                    ins = tt(four(BV(h)), ps, c4(C_BETA, g))
                elif kind == "KK":
                    dve.wait_ge(mask_ok, 4 * p + 2 * h + 2)
                    link(tt(four(X(h)), ps, four(XT(h))))
                    ins = tt(four(X(h)), four(X(h)), c4(C_BETA, g))
                elif kind == "LT":
                    link(nc.vector.tensor_copy(LT(h), k.bank(n % BANKS)))
                    link(nc.vector.scalar_tensor_tensor(out=four(XT(h)), in0=ps, scalar=-1.0, in1=mask4(level[:, 0:P]), op0=ALU.mult, op1=ALU.mult))
                    link(tt(four(XT(h)), four(XT(h)), mask4(k.const("ident")), ALU.add))
                    link(nc.vector.scalar_tensor_tensor(out=four(X(h)), in0=four(X(h)), scalar=-1.0, in1=mask4(levelT), op0=ALU.mult, op1=ALU.mult))
                    ins = tt(four(X(h)), four(X(h)), mask4(k.const("ident")), ALU.add)
                elif kind == "AT":
                    dve.wait_ge(mask_ok, 4 * p + 2 * h + 1)
                    dve.wait_ge(exp_ok, exps_before(p, h) + 3)
                    link(nc.vector.scalar_tensor_tensor(out=keep(g, "QD"), in0=qs(g - 2), scalar=SCALE, in1=keep(g, "QD"), op0=ALU.mult, op1=ALU.mult))
                    ins = nc.vector.scalar_tensor_tensor(out=keep(g, "AT"), in0=k.bank(n % BANKS), scalar=SCALE, in1=DD(h), op0=ALU.mult, op1=ALU.mult)
                elif kind == "XT":
                    ins = tt(XT(h), XT(h), k.bank(n % BANKS), ALU.subtract)
                ins.then_inc(dve_out, 1)


def gdn_chunks_phase(k, d, cp, keep, y, own):
    nc = k.nc
    col = k.pl(cp)
    S = lambda n, h: k.pl(own[n % 4])[:, h * P:(h + 1) * P]
    VN = lambda n, h: k.pl(own[4 + (n // 2) % 2])[:, h * P:(h + 1) * P]
    ctx_n, lat_n = CTX // CHUNK, T // CHUNK
    NCH = ctx_n + lat_n

    def place(n, h):
        if n < ctx_n:
            c = n if d == 0 else ctx_n - 1 - n
            return h // 2, 2 * (h % 2) + c // 2, c % 2
        c = n - ctx_n if d == 0 else NCH - 1 - n
        return 2 + h, c // 2, c % 2

    u_ok, vn_ok, ds_ok, st_ok, o_ok, o_out = (k.sem(f"h{d}_{x}") for x in ("u_ok", "vn_ok", "ds_ok", "st_ok", "o_ok", "o_out"))
    outs = [n for n in range(ctx_n, NCH) if n % 2 == 1]
    with nc.Block() as block:
        @block.tensor
        def _(pe):
            for n in range(NCH):
                for h in range(4):
                    g, s, hf = place(n, h)
                    lo = 64 * hf
                    pe.wait_ge(st_ok, 4 * n + h + 1)
                    if n - 1 in outs:
                        pe.wait_ge(o_out, 4 * outs.index(n - 1) + h + 1)
                    nc.tensor.matmul(k.bank(h)[lo:lo + 64, 0:P], keep(g, "W")[:, s * P + lo:s * P + lo + 64], S(n, h),
                                     start=True, stop=True).then_inc(u_ok, 1)
                if n < NCH - 1:
                    for h in range(4):
                        g, s, hf = place(n, h)
                        rows = slice(64 * hf, 64 * hf + 64)
                        pe.wait_ge(vn_ok, 4 * n + h + 1)
                        nc.tensor.matmul(k.bank(4 + h)[:, 0:P], keep(g, "KD")[rows, s * P:(s + 1) * P], VN(n, h)[rows, :],
                                         start=True, stop=True).then_inc(ds_ok, 1)
                if n in outs:
                    m = outs.index(n)
                    for h in range(4):
                        g, s, _ = place(n, h)
                        pe.wait_ge(vn_ok, 4 * n + h + 1)
                        o = k.bank(h)[:, 0:P]
                        for q, nn in enumerate((n - 1, n)):
                            lo = 64 * place(nn, h)[2]
                            nc.tensor.matmul(o[:, lo:lo + 64], S(nn, h), keep(g, "QD")[:, s * P + lo:s * P + lo + 64],
                                             start=(q == 0), stop=False, skip_group_check=True)
                        nc.tensor.matmul(o, VN(n, h), keep(g, "AT")[:, s * P:(s + 1) * P], start=False, stop=True,
                                         skip_group_check=True).then_inc(o_ok, 1)

        @block.vector
        def _(dve):
            for h in range(4):
                nc.vector.memset(S(0, h), 0.0).then_inc(st_ok, 1)
            for n in range(NCH):
                for h in range(4):
                    g, s, hf = place(n, h)
                    rows = slice(64 * hf, 64 * hf + 64)
                    dve.wait_ge(u_ok, 4 * n + h + 1)
                    nc.vector.tensor_tensor(VN(n, h)[rows, :], keep(g, "U0")[rows, s * P:(s + 1) * P], k.bank(h)[rows, 0:P],
                                            ALU.subtract).then_inc(vn_ok, 1)
                if n < NCH - 1:
                    for h in range(4):
                        g, s, hf = place(n, h)
                        c = C_END + 48 * hf + gdn_col(d, g) + s
                        dve.wait_ge(ds_ok, 4 * n + h + 1)
                        dve.wait_ge(st_ok, 4 * n + h + 1)
                        nc.vector.scalar_tensor_tensor(out=S(n + 1, h), in0=S(n, h), scalar=col[:, c:c + 1], in1=k.bank(4 + h)[:, 0:P],
                                                       op0=ALU.mult, op1=ALU.add).then_inc(st_ok, 1)
                if d == 1 and n in outs:
                    m = outs.index(n)
                    for h in range(4):
                        s = place(n, h)[1]
                        o = k.pl(y + h)[:, s * P:(s + 1) * P]
                        dve.wait_ge(o_ok, 4 * m + h + 1)
                        nc.vector.tensor_tensor(o, o, k.bank(h)[:, 0:P], ALU.add).then_inc(o_out, 1)

        if d == 0:
            @block.scalar
            def _(act):
                for m, n in enumerate(outs):
                    for h in range(4):
                        s = place(n, h)[1]
                        act.wait_ge(o_ok, 4 * m + h + 1)
                        nc.scalar.activation(k.pl(y + h)[:, s * P:(s + 1) * P], k.bank(h)[:, 0:P], ACT.Copy).then_inc(o_out, 1)


def route_phase(k, lg, aff, work, msk, slot_t):
    nc = k.nc
    E = 16
    rounds = 2 * T // E // 8
    mx, sm = k.small[:, 0:4], k.small[:, 4:8]
    m8 = k.small[0:E, 8:16]
    ones = k.pl(msk + 1)[0:E, :]
    A, W, M = k.pl(aff)[0:E, :], k.pl(work)[0:E, :], k.pl(msk)[0:E, :]
    sub_ok, e_ok, a_ok, t_ok, s_ok, back = (k.sem(f"t_{x}") for x in ("sub_ok", "e_ok", "a_ok", "t_ok", "s_ok", "back"))
    bc = lambda x: x.unsqueeze(2).broadcast_to([P, TT, E])
    with nc.Block() as block:
        @block.vector
        def _(dve):
            link = lambda ins: k.dve_chain(dve, ins)
            link(nc.vector.tensor_reduce(mx, lg, AX.X, ALU.max))
            nc.vector.tensor_tensor(lg, lg, bc(mx), ALU.subtract).then_inc(sub_ok, 1)
            dve.wait_ge(e_ok, 1)
            link(nc.vector.tensor_reduce(sm, lg, AX.X, ALU.add))
            link(nc.vector.reciprocal(sm, sm))
            nc.vector.tensor_tensor(lg, lg, bc(sm), ALU.mult).then_inc(a_ok, 1)
            dve.wait_ge(t_ok, 1)
            link(nc.vector.tensor_copy(W, k.bank(0)[0:E, :]))
            for _ in range(rounds):
                link(nc.vector.max(m8, W))
                link(nc.vector.match_replace(W, m8, W, -1.0))
            link(nc.vector.tensor_scalar(M, W, -1.0, None, ALU.is_equal))
            link(nc.vector.memset(ones, 1.0))
            link(nc.vector.tensor_tensor_scan(W, ones, M, 0.0, ALU.mult, ALU.add))
            link(nc.vector.tensor_tensor(W, W, M, ALU.mult))
            nc.vector.tensor_scalar(W, W, -1.0, None, ALU.add).then_inc(s_ok, 1)
            dve.wait_ge(back, 1)
            link(nc.vector.tensor_copy(slot_t, k.bank(1)[:, 0:TT * E].rearrange("p (i e) -> p i e", e=E)))

        @block.scalar
        def _(act):
            act.wait_ge(sub_ok, 1)
            nc.scalar.activation(lg, lg, ACT.Exp).then_inc(e_ok, 1)

        @block.tensor
        def _(pe):
            pe.wait_ge(a_ok, 1)
            for i in range(TT):
                ins = nc.tensor.transpose(k.bank(0)[0:E, i * P:(i + 1) * P], lg[:, i, :], k.const("ident"))
            ins.then_inc(t_ok, 1)
            pe.wait_ge(s_ok, 1)
            for i in range(TT):
                ins = nc.tensor.transpose(k.bank(1)[:, i * E:(i + 1) * E], W[:, i * P:(i + 1) * P], k.const("ident")[0:E, 0:E])
            ins.then_inc(back, 1)


def gather_phase(k, lg, slot_t, sel, ht, xe, gt):
    nc = k.nc
    pl = k.pl
    selv = pl(sel, 8).rearrange("p (i e s) -> p i e s", i=TT, e=16)
    self_ = pl(sel, 8).rearrange("p (i c) -> p i c", i=TT)
    htv = pl(ht, 8).rearrange("p (i c) -> p i c", i=TT)
    sel_ok, t_ok, t_out, x_ok, x_out, g_ok, gt_ok, gt_out = (k.sem(f"x_{s}") for s in ("sel_ok", "t_ok", "t_out", "x_ok", "x_out", "g_ok", "gt_ok", "gt_out"))
    bc = lambda x: x.unsqueeze(2).broadcast_to([P, 16, 64])
    iota = k.const("iota")[:, 0:64].unsqueeze(1).broadcast_to([P, 16, 64])
    with nc.Block() as block:
        @block.vector
        def _(dve):
            for i in range(TT):
                nc.vector.tensor_tensor(selv[:, i], iota, bc(slot_t[:, i, :]), ALU.is_equal).then_inc(sel_ok, 1)
            for n in range(0, 16, 2):
                dve.wait_ge(x_ok, n + 1)
                nc.vector.tensor_copy(pl(xe + n), k.bank(n % 4)).then_inc(x_out, 1)
            dve.wait_ge(x_ok, 16)
            for i in range(TT):
                nc.vector.tensor_tensor(selv[:, i], selv[:, i], bc(lg[:, i, :]), ALU.mult).then_inc(g_ok, 1)

        @block.tensor
        def _(pe):
            for n in range(8):
                if n >= 4:
                    pe.wait_ge(t_out, n - 3)
                for c in range(4):
                    ins = nc.tensor.transpose(k.bank(4 + n % 4)[:, c * P:(c + 1) * P], pl(H_PL + 4 * (n % 2) + c)[:, (n // 2) * P:(n // 2 + 1) * P], k.const("ident"))
                ins.then_inc(t_ok, 1)
            pe.wait_ge(sel_ok, TT)
            pe.wait_ge(t_out, 8)
            for n in range(16):
                c, half = n // 2, n % 2
                if n >= 4:
                    pe.wait_ge(x_out if n % 2 == 0 else gt_out, (n - 4) // 2 + 1)
                for i in range(TT):
                    ins = nc.tensor.matmul(k.bank(n % 4), htv[:, i, c * P:(c + 1) * P], self_[:, i, half * 512:half * 512 + 512], start=(i == 0), stop=(i == 3))
                ins.then_inc(x_ok, 1)
            pe.wait_ge(g_ok, TT)
            for e in range(8):
                if e >= 4:
                    pe.wait_ge(gt_out, 8 + e - 3)
                for i in range(TT):
                    ins = nc.tensor.transpose(k.bank(4 + e % 4)[:, i * P:(i + 1) * P], self_[:, i, e * P:(e + 1) * P], k.const("ident"))
                ins.then_inc(gt_ok, 1)

        @block.scalar
        def _(act):
            for n in range(8):
                act.wait_ge(t_ok, n + 1)
                nc.scalar.activation(htv[:, n // 2, (n % 2) * 512:(n % 2) * 512 + 512], k.bank(4 + n % 4), ACT.Copy).then_inc(t_out, 1)
            for n in range(1, 16, 2):
                act.wait_ge(x_ok, n + 1)
                nc.scalar.activation(pl(xe + n), k.bank(n % 4), ACT.Copy).then_inc(gt_out, 1)
            for e in range(8):
                act.wait_ge(gt_ok, e + 1)
                nc.scalar.activation(pl(gt + e), k.bank(4 + e % 4), ACT.Copy).then_inc(gt_out, 1)


def expert_order():
    order = []
    for p in range(PAIRS + 1):
        if p < PAIRS:
            order += [(m, 2 * p + e, q) for e in range(2) for m in ("w_gate", "w_up") for q in range(8)]
        if p >= 1:
            order += [("w_down", 2 * (p - 1) + e, q) for e in range(2) for q in range(8)]
    return order


def expert_source(k, m, e, q):
    return k.dram[m][e, q * P:(q + 1) * P, :]


def spare_slots_phase(k, spare):
    nc = k.nc
    k.spare = spare
    k.spare_in = [k.sem(f"spare_in{i}") for i in range(len(spare))]
    with nc.Block() as block:
        @block.sync
        def _(sp):
            for i, piece in enumerate(expert_order()[RING:RING + len(spare)]):
                sp.dma_start(k.pl(spare[i], 2), expert_source(k, *piece)).then_inc(k.spare_in[i], 16)


def experts_phase(k, xe, hid, hid_t, ye, gt, x, scale, following=()):
    nc = k.nc
    pl = k.pl
    base = k.pieces
    order = expert_order()
    SLOTS = RING + len(k.spare_in)

    def slot(g):
        n = (g - base) % SLOTS
        return k.pl(RING_PL + 2 * ((base + n) % RING) if n < RING else k.spare[n - RING], 2)

    def loaded(g):
        n, turn = (g - base) % SLOTS, (g - base) // SLOTS
        if n < RING:
            return k.loaded[(base + n) % RING], 16 * ((base + n) // RING + 1 + turn)
        return k.spare_in[n - RING], 16 * (turn + 1)

    gu_ok, silu_ok, hid_ok, t_ok, t_out, y_ok, y_out = (k.sem(f"e_{s}") for s in ("gu_ok", "silu_ok", "hid_ok", "t_ok", "t_out", "y_ok", "y_out"))
    sc_ok, sc_out = k.sem("e_sc_ok"), k.sem("e_sc_out")
    k.pieces_end = base + len(order)
    H = lambda p: pl(hid + 2 * (p % 2), 2)
    HT = lambda p: pl(hid_t + 2 * (p % 2), 2)
    xev = lambda q, e: pl(xe + 2 * q, 2)[:, e * 64:e * 64 + 64]
    with nc.Block() as block:
        @block.sync
        def _(sp):
            for i, (m, e, q) in enumerate(order):
                g = base + i
                if i < k.ahead or RING <= i < SLOTS:
                    continue
                if i >= SLOTS:
                    sp.wait_ge(k.piece_done, g - SLOTS + 1)
                sp.dma_start(slot(g), expert_source(k, m, e, q)).then_inc(loaded(g)[0], 16)

        @block.tensor
        def _(pe):
            g = base

            def scatter(u, c):
                if c == 0:
                    pe.wait_ge(y_out, u + 1)
                    pe.wait_ge(t_out, PAIRS if u == PAIRS - 2 else u + 1)
                if c >= 2 or u >= 1:
                    pe.wait_ge(sc_out, 8 * u + max(c - 1, 0))
                nc.tensor.matmul(k.bank(4 + c % 2), k.pl(ye + 2 * u, 2)[:, c * P:(c + 1) * P], k.pl(gt + u), start=True, stop=True).then_inc(sc_ok, 1)

            for p in range(PAIRS + 2):
                if p < PAIRS:
                    if p >= 1:
                        pe.wait_ge(hid_ok, p)
                    for e in range(2):
                        rows = slice(64 * e, 64 * e + 64)
                        for b in (0, 2):
                            for q in range(8):
                                pe.wait_ge(*loaded(g))
                                for f in range(2):
                                    ins = nc.tensor.matmul(k.bank(b + f)[rows, :], xev(q, 2 * p + e), slot(g)[:, f * 512:f * 512 + 512],
                                                           start=(q == 0), stop=(q == 7))
                                ins.then_inc(k.piece_done, 1)
                                g += 1
                                n = e * 16 + b // 2 * 8 + q
                                if p >= 2 and n % 4 == 3:
                                    scatter(p - 2, n // 4)
                    pe.wait_ge(k.piece_done, g)
                    nc.tensor.nop().then_inc(gu_ok, 1)
                if 1 <= p <= PAIRS:
                    u = p - 1
                    pe.wait_ge(hid_ok, u + 1)
                    if u >= 1:
                        pe.wait_ge(sc_out, 8 * min(u, PAIRS - 2))
                    if u >= 1:
                        pe.wait_ge(t_out, u)
                    for f in range(8):
                        ins = nc.tensor.transpose(k.bank(4 + f // 4)[:, (f % 4) * P:(f % 4 + 1) * P], H(u)[:, f * P:(f + 1) * P], k.const("ident"))
                    ins.then_inc(t_ok, 1)
                    pe.wait_ge(t_out, u + 1)
                    if u >= 1:
                        pe.wait_ge(y_out, u)
                    for e in range(2):
                        rows = slice(64 * e, 64 * e + 64)
                        for q in range(8):
                            pe.wait_ge(*loaded(g))
                            for f in range(2):
                                ins = nc.tensor.matmul(k.bank(6 + f)[rows, :], HT(u)[:, q * P + 64 * e:q * P + 64 * e + 64], slot(g)[:, f * 512:f * 512 + 512],
                                                       start=(q == 0), stop=(q == 7))
                            ins.then_inc(k.piece_done, 1)
                            g += 1
                    pe.wait_ge(k.piece_done, g)
                    nc.tensor.nop().then_inc(y_ok, 1)
                if p >= PAIRS:
                    for c in range(8):
                        scatter(p - 2, c)

        @block.scalar
        def _(act):
            for p in range(PAIRS + 1):
                if p < PAIRS:
                    act.wait_ge(gu_ok, p + 1)
                    if p >= 2:
                        act.wait_ge(t_ok, p - 1)
                    for f in range(2):
                        nc.scalar.activation(H(p)[:, f * 512:f * 512 + 512], k.bank(f), ACT.Silu).then_inc(silu_ok, 1)
                if p >= 1:
                    u = p - 1
                    act.wait_ge(t_ok, u + 1)
                    nc.scalar.activation(HT(u)[:, 0:512], k.bank(4), ACT.Copy)
                    nc.scalar.activation(HT(u)[:, 512:1024], k.bank(5), ACT.Copy).then_inc(t_out, 1)
                    act.wait_ge(y_ok, u + 1)
                    nc.scalar.activation(pl(ye + 2 * u), k.bank(6), ACT.Copy)
                    nc.scalar.activation(pl(ye + 2 * u + 1), k.bank(7), ACT.Copy).then_inc(y_out, 1)

        @block.vector
        def _(dve):
            for p in range(PAIRS + 2):
                if p >= 2:
                    u = p - 2
                    for c in range(8):
                        dve.wait_ge(sc_ok, 8 * u + c + 1)
                        if u >= 1:
                            dve.wait_ge(sc_out, 8 * (u - 1) + c + 1)
                        nc.vector.scalar_tensor_tensor(out=k.pl(x + c), in0=k.bank(4 + c % 2), scalar=scale(c), in1=k.pl(x + c),
                                                       op0=ALU.mult, op1=ALU.add).then_inc(sc_out, 1)
                if p < PAIRS:
                    for f in range(2):
                        dve.wait_ge(silu_ok, 2 * p + f + 1)
                        h = H(p)[:, f * 512:f * 512 + 512]
                        ins = nc.vector.tensor_tensor(h, h, k.bank(2 + f), ALU.mult)
                    ins.then_inc(hid_ok, 1)

    k.pieces += len(order)
    k.ahead = 0


def silu_c_phase(k):
    nc, cc = k.nc, k.small[:, 0:16]
    with nc.Block() as block:
        @block.scalar
        def _(act):
            k.act_chain(act, nc.scalar.activation(cc[:, 0::2], k.col("c_2", 0, 8), ACT.Silu))
            k.act_chain(act, nc.scalar.activation(cc[:, 1::2], k.col("c_ctx_2", 0, 8), ACT.Silu))


def mod_products(k, acc, parts):
    nc = k.nc
    COLS_ = 1024
    slots = 4
    steps = [(t, q) for t in parts for q in range(KT)]
    w = lambda n: k.pl(MRG_PL + 2 * (n % slots), 2)

    def gpsimd(pool):
        mod_in = [k.sem(f"mod_in{parts[0]}_{i}") for i in range(slots)]
        for n in range(len(steps) + slots - 1):
            if n < len(steps):
                t, q = steps[n]
                pool.dma_start(w(n), k.dram["w_mod"][q * P:(q + 1) * P, t * COLS_:(t + 1) * COLS_]).then_inc(mod_in[n % slots], 16)
            m = n - slots + 1
            if m >= 0:
                t, q = steps[m]
                pool.wait_ge(mod_in[m % slots], 16 * (m // slots + 1))
                for who in ((1, 0) if t < 2 else (0,)):
                    a = k.pl(acc + 12 * who + 2 * t, 2)
                    c = k.small[:, 2 * q + who:2 * q + who + 1]
                    o = a if q == 0 else k.pl(acc + 16, 2) if who else w(m)
                    k.pool_chain(pool, nc.gpsimd.tensor_scalar(o, w(m), c, None, ALU.mult))
                    if q > 0:
                        k.pool_chain(pool, nc.gpsimd.tensor_tensor(a, a, o, ALU.add))

    return gpsimd


def mod_sum_phase(k, acc):
    nc = k.nc
    summed = k.sem("mod_summed")
    with nc.Block() as block:
        @block.tensor
        def _(pe):
            for i in range(64):
                ins = nc.tensor.matmul(k.bank(0)[:, i:i + 1], k.pl(acc, 16)[:, i * P:(i + 1) * P], k.const("ones")[:, 0:1], start=True, stop=True)
            ins.then_inc(summed, 1)

        @block.vector
        def _(dve):
            dve.wait_ge(summed, 1)
            k.dve_chain(dve, nc.vector.tensor_tensor(k.mods[:, 0:96:2], k.bank(0)[:, 0:48], k.col("b_mod_2", 0, 48), ALU.add))
            k.dve_chain(dve, nc.vector.tensor_tensor(k.mods[:, 1:32:2], k.bank(0)[:, 48:64], k.col("b_mod_2", 0, 16), ALU.add))


def program(nc, dr, out, stage):
    with ExitStack() as ctx:
        k = Core(nc, ctx, dr)
        order(k, dr, out, stage)
        run_plan(k)


def order(k, dr, out, stage):
    if True:
        nc = k.nc
        pl = k.pl
        plan(k, load_phase, k, [(k.params[:, :], dr["params"]), (k.cst[:, :], dr["consts"])]
                   + [(pl(WORK + c), dr["x"][c * P:(c + 1) * P, :]) for c in range(KT)])
        H = lambda c: pl(H_PL + c)
        plan(k, rms_phase, k, lambda c: pl(WORK + c), H, lambda c: k.col("norm_mix", c), WORK + 8)

        def dump(first, n=8):
            plan(k, load_phase, k, [(out[c * P:(c + 1) * P, :], pl(first + c)) for c in range(n)], k.out_done)

        if stage == "h":
            return dump(H_PL)

        def tiles(first, n, dst, **more):
            return [job(wtile(dr["w_in"], first + i), H, "A", pl(dst + i), **more) for i in range(n)]

        def convs(first, n, dst, wname, bname, taps, post=None, c0=0, nch=None):
            js = []
            for i in range(n):
                t = [(k.col(wname, (taps - 1 - s) * nch + c0 + i), s) for s in range(taps)]
                js.append(job(wtile(dr["w_in"], first + i), H, "D", pl(dst + i), taps=t,
                              bias=k.col(bname, c0 + i) if bname else None, post=post))
            return js

        silu = [(0, P, ACT.Silu)]

        def merge(y, m):
            js = []
            for c in range(KT):
                g = pl(WORK + c)
                js.append(job(wtile(dr["w_in"], W_GATE + 8 * m + c), H, "A", g, func=ACT.Sigmoid, signal=True))
                js.append(job(wtile(dr["w_branch"], 8 * m + c), lambda q: pl(y + q), "D", pl(MRG_PL + c), gate=g,
                              first=(m == 0), needs=len(js) - 1))
            plan(k, project_phase, k, js)

        z, xs, bt, ct, dt, w = WORK, WORK + 8, WORK + 16, WORK + 20, WORK + 24, WORK + 25
        js = tiles(W_Z, 8, z, func=ACT.Silu)
        js += convs(W_XBC, 16, xs, "ssm_conv_w", "ssm_conv_b", 4, silu, nch=16)
        js.append(job([(dr["w_dt"], 0, 8)], H, "A", pl(dt)[0:16, :], m=16))
        plan(k, project_phase, k, js)
        plan(k, mamba_phase, k, z, xs, bt, ct, dt, w)
        ym = w
        if stage == "mambaraw":
            return dump(ym)
        plan(k, rms_phase, k, lambda c: pl(ym + c), lambda c: pl(WORK + 8 + c), lambda c: k.col("ssm_norm", c), ym + 8)
        if stage == "mamba":
            return dump(WORK + 8)
        merge(WORK + 8, 0)
        if stage == "merge0":
            return dump(MRG_PL)

        g, r, i, th, xc = WORK + 8, WORK, WORK + 16, WORK + 24, WORK + 32
        plan(k, project_phase, k, tiles(W_LG, 8, g, func=ACT.Gelu_apprx_tanh)
                      + convs(W_LX, 8, xc, "lru_conv_w", "lru_conv_b", 4, nch=8))
        js = []
        for c in range(8):
            for wn, bn, dst in (("lru_w_a", "lru_b_a", r), ("lru_w_i", "lru_b_i", i)):
                js.append(job([(dr[wn][:, c * P:(c + 1) * P], 0, 1)], lambda q, c=c: pl(xc + c), "A", pl(dst + c),
                              func=ACT.Sigmoid, bias=k.col(bn, c)))
        plan(k, project_phase, k, js)
        plan(k, lru_phase, k, g, xc, r, i, th)
        if stage == "lru":
            return dump(g)
        merge(g, 1)

        q, kk, v, y, g, cos, sin, table, w = WORK, WORK + 4, WORK + 16, WORK + 8, WORK + 24, WORK + 32, WORK + 33, WORK + 34, WORK + 42
        js = tiles(W_RQ, 8, q)
        for i in range(8):
            dst = pl(v, 8).rearrange("p (t c) -> p t c", c=D)[:, :, i * P:(i + 1) * P]
            js.append(job(wtile(dr["w_in"], W_RV + i), H, "A", dst, swap=True))
        js += tiles(W_RG, 8, g, func=ACT.Silu)
        plan(k, load_phase, k, [(pl(cos), dr["cos"]), (pl(sin), dr["sin"]), (pl(table, 8), dr["ret_table"])])
        plan(k, project_phase, k, js)
        plan(k, ret_phase, k, q, kk, v, g, y, cos, sin, table, w)
        if stage == "ret":
            return dump(y)
        merge(y, 2)

        plan(k, load_phase, k, [(dr["spill"][c], pl(MRG_PL + c)) for c in range(8)])
        rr, kk, vv, sg, aa, lora, rows, w = WORK, WORK + 8, WORK + 16, WORK + 24, WORK + 32, WORK + 40, WORK + 42, WORK + 43
        omm = k.small[:, 130:156]
        plan(k, columns_phase, k, [lambda: nc.vector.tensor_scalar(omm, k.col("rwkv_mu", 0, 26), -1.0, 1.0, ALU.mult, ALU.add)])
        js = []
        for i in range(26):
            post = {24: [(0, 64, ACT.Tanh)], 25: [(0, P, ACT.Sigmoid)]}.get(i)
            js.append(job(wtile(dr["w_in"], W_RW + i), H, "D", pl((WORK + i) if i < 24 else lora + i - 24),
                          taps=[(omm[:, i:i + 1], 0), (k.col("rwkv_mu", i), 1)], post=post))
        plan(k, project_phase, k, js)
        js = []
        for c in range(8):
            for wn, bn, dst in (("lora_w", "rwkv_w0", sg), ("lora_a", "rwkv_a0", aa)):
                js.append(job([(dr[wn][:, c * P:(c + 1) * P], 0, 1)], lambda q: pl(lora), "A", pl(dst + c),
                              func=ACT.Sigmoid, bias=k.col(bn, c)))
        plan(k, project_phase, k, js)
        plan(k, rwkv_prepare_phase, k, rr, kk, vv, sg, aa, rows, w)
        plan(k, rwkv_core_phase, k, rr, kk, vv, sg, aa, w, ring=True)
        plan(k, rwkv_finish_phase, k, rr, vv, rows, w)
        plan(k, project_phase, k, [job([(dr["lora_g"][:, c * P:(c + 1) * P], 0, 1)], lambda q: pl(lora + 1), "D", pl(WORK + 8 + c),
                              times=pl(rr + c)) for c in range(8)])
        if stage == "rwkv":
            return dump(WORK + 8)
        plan(k, load_phase, k, [(pl(MRG_PL + c), dr["spill"][c]) for c in range(8)])
        merge(WORK + 8, 3)

        plan(k, k.recycle)
        X = WORK
        plan(k, load_phase, k, [(pl(X + c), dr["x"][c * P:(c + 1) * P, :]) for c in range(KT)])
        plan(k, project_phase, k, [job(wtile(dr["w_out"], c), lambda q: pl(MRG_PL + q), "D", pl(X + c), add=pl(X + c)) for c in range(KT)])
        if stage == "mixed":
            return dump(X)
        plan(k, rms_phase, k, lambda c: pl(X + c), H, lambda c: k.col("norm_ffn", c), WORK + 8)
        hid, tmp, acc = WORK + 18, WORK + 40, WORK + 41
        plan(k, silu_c_phase, k)
        js = []
        for i in range(FT):
            t = lambda c: [(k.col("ffn_conv_w", (2 - s) * 44 + c), s) for s in range(3)]
            js.append(job(wtile(dr["ffn_up"], FT + i), H, "D", pl(hid + i), taps=t(FT + i),
                          bias=k.col("ffn_conv_b", FT + i), post=silu))
            js.append(job(wtile(dr["ffn_up"], i), H, "D", pl(tmp), taps=t(i), bias=k.col("ffn_conv_b", i),
                          mul=pl(hid + i), needs=len(js) - 1))
        plan(k, project_phase, k, js, beside=mod_products(k, acc, range(0, 4)))
        plan(k, project_phase, k, [job(wtile(dr["ffn_down"], c, FT), lambda q: pl(hid + q), "D", pl(X + c), add=pl(X + c)) for c in range(KT)],
             beside=mod_products(k, acc, range(4, 6)))
        plan(k, rms_phase, k, lambda c: pl(X + c), lambda c: pl(X + c), lambda c: k.col("norm_final", c), WORK + 8)
        if stage == "first":
            return dump(X)

        second_block(k, dr, out, stage, X, dump, acc)


def second_block(k, dr, out, stage, X, dump, acc):
    nc, pl = k.nc, k.pl
    H = lambda c: pl(H_PL + c)
    plan(k, mod_sum_phase, k, acc)
    mod = lambda part, c, who=0: k.mods[:, 2 * (8 * part + c) + who:2 * (8 * part + c) + who + 1]
    mods = lambda part, who: k.mods[:, 16 * part + who:16 * part + 16:2]
    SH1, SC1, GT1, SH2, SC2, GT2 = range(6)
    wl, wc, wf = (k.mods[:, 96 + 8 * n:104 + 8 * n] for n in range(3))
    mul = lambda o, part, who, name: (lambda: nc.vector.scalar_tensor_tensor(out=o, in0=mods(part, who), scalar=1.0,
                                                                             in1=k.col(name, 0, 8), op0=ALU.add, op1=ALU.mult))
    plan(k, columns_phase, k, [mul(wl, SC1, 0, "norm_mix_2"), mul(wc, SC1, 1, "norm_mix_2"), mul(wf, SC2, 0, "norm_ffn_2")])
    plan(k, rms_phase, k, lambda c: pl(X + c), H, lambda c: wl[:, c:c + 1], WORK + 8, shift=lambda c: mod(SH1, c))
    if stage == "h2":
        return dump(H_PL)
    Hc = lambda c: pl(MRG_PL, 4)[:, c * CTX:(c + 1) * CTX]
    plan(k, load_phase, k, [(Hc(c), dr["ctx"][c * P:(c + 1) * P, :]) for c in range(KT)])
    plan(k, rms_phase, k, Hc, Hc, lambda c: wc[:, c:c + 1], WORK + 8, n=CTX, shift=lambda c: mod(SH1, c, 1))

    GQ, GATE, NQ, NKK, NV = WORK + 8, WORK + 20, WORK + 24, WORK + 28, WORK + 32
    CK, NKC, NVC, Y, w = WORK + 36, WORK + 40, WORK + 42, WORK + 44, WORK + 52
    ab = k.small[:, 128:128 + 96].rearrange("p (t m) -> p t m", m=16)
    half = lambda base, c: pl(base + c // 2)[:, (c % 2) * CTX:(c % 2 + 1) * CTX]
    vt = pl(NV, 4).rearrange("p (t c) -> p t c", c=T)
    vct = pl(NVC, 2).rearrange("p (t c) -> p t c", c=T)
    silu = [(0, P, ACT.Silu)]
    five = lambda c: [(k.col("conv_qkv_2", j * 12 + c), 2 - j) for j in (2, 0, 1, 3, 4)]
    js = [job(wtile(dr["w_in_2"], c), H, "D", pl(GQ + c), taps=five(c), post=silu) for c in range(12)]
    js += [job(wtile(dr["w_in_2"], 12 + c), H, "A", pl(GATE + c), func=ACT.Silu) for c in range(4)]
    js += [job(wtile(dr["w_in_2"], 16 + c), H, "A", pl(NQ + c)) for c in range(8)]
    js += [job(wtile(dr["w_in_2"], 24 + c), H, "A", vt[:, :, c * P:(c + 1) * P], swap=True) for c in range(4)]
    js.append(job([(dr["w_ab"], 0, 8)], H, "A", ab[:, 0:4, :], m=16, swap=True))
    js += [job(wtile(dr["w_in_2"], 4 + c), Hc, "D", half(CK, c), n=CTX, taps=five(4 + c), post=silu) for c in range(8)]
    js += [job(wtile(dr["w_in_2"], 20 + c), Hc, "A", half(NKC, c), n=CTX) for c in range(4)]
    js += [job(wtile(dr["w_in_2"], 24 + c), Hc, "A", vct[:, :, c * P:(c + 1) * P], n=CTX, swap=True) for c in range(4)]
    js.append(job([(dr["w_ab"], 0, 8)], Hc, "A", ab[:, 4:6, :], m=16, n=CTX, swap=True))
    plan(k, project_phase, k, js)
    kc = pl(NKC, 2).rearrange("p (c t) -> p c t", t=CTX)
    plan(k, attention_phase, k, NQ, NKK, vt, kc, vct, Y + 4, H_PL)
    if stage == "na":
        plan(k, load_phase, k, [(out[c * P:(c + 1) * P, :], pl(Y + 4 + c % 4)) for c in range(8)], k.out_done)
        return

    plan(k, k.recycle)
    cos, sin = NQ, NQ + 1
    plan(k, load_phase, k, [(pl(cos), dr["cos2"]), (pl(sin), dr["sin2"])])
    plan(k, l2_rope_phase, k, "lq", [pl(GQ + c) for c in range(8)], T, H_PL, pl(cos), pl(sin))
    plan(k, l2_rope_phase, k, "lk", [half(CK, c) for c in range(4)], CTX, H_PL)
    free = ([NQ + n for n in range(12)] + [NKC + n for n in range(4)] + [H_PL + n for n in range(16)]
            + [RING_PL + n for n in range(2 * RING)] + [w + n for n in range(7)])
    cp, own, kept = free[0], free[1:17], free[17:]
    plan(k, gdn_columns_phase, k, ab, cp, free[1], ring=True)
    names = [(g, x) for g in range(6) for x in (("W", "U0", "KD") if g < 2 else ("W", "U0", "KD", "QD", "AT"))]
    keep = lambda g, x: pl(kept[names.index((g, x))])
    kh = lambda ctx, h: half(CK, h) if ctx else pl(GQ + 4 + h)
    vh = lambda ctx, h: half(CK, 4 + h) if ctx else pl(GQ + 8 + h)
    for d in range(2):
        plan(k, gdn_make_phase, k, d, lambda h: pl(GQ + h), kh, vh, cp, keep, own, ring=True)
        plan(k, gdn_chunks_phase, k, d, cp, keep, Y, own, ring=True)
    plan(k, l2_rope_phase, k, "ln", [pl(Y + c) for c in range(4)], T, H_PL, mean=1.0 / P,
                  finish=lambda c: nc.vector.scalar_tensor_tensor(out=pl(Y + c), in0=pl(Y + c), scalar=k.col("gdn_norm_2"),
                                                                  in1=pl(GATE + c), op0=ALU.mult, op1=ALU.mult))
    if stage == "gdn":
        plan(k, load_phase, k, [(out[c * P:(c + 1) * P, :], pl(Y + c % 4)) for c in range(8)], k.out_done)
        return
    plan(k, project_phase, k, [job(wtile(dr["w_out_2"], c), lambda q: pl(Y + q), "D", pl(X + c), scale=mod(GT1, c), add=pl(X + c)) for c in range(KT)])
    if stage == "x2":
        return dump(X)

    plan(k, k.recycle)
    plan(k, spare_slots_phase, k, [MRG_PL + 2 * i for i in range(4)] + [WORK + 52 + 2 * i for i in range(3)])
    plan(k, rms_phase, k, lambda c: pl(X + c), H, lambda c: wf[:, c:c + 1], WORK + 8, shift=lambda c: mod(SH2, c))
    if stage == "hmoe":
        return dump(H_PL)
    lg = k.small[:, 128:192].rearrange("p (i e) -> p i e", e=16)
    slot_t = k.small[:, 192:256].rearrange("p (i e) -> p i e", e=16)
    plan(k, project_phase, k, [job([(dr["w_router"], 0, 8)], H, "A", lg, m=16, swap=True)])
    plan(k, route_phase, k, lg, WORK + 8, WORK + 9, WORK + 10, slot_t)
    sel, ht, xe, gt, hid = WORK + 8, WORK + 16, WORK + 24, WORK + 40, WORK + 48
    plan(k, gather_phase, k, lg, slot_t, sel, ht, xe, gt)
    plan(k, experts_phase, k, xe, hid, H_PL, sel, gt, X, lambda c: mod(GT2, c))
    plan(k, rms_phase, k, lambda c: pl(X + c), lambda c: pl(X + c), lambda c: k.col("final_norm_2", c), WORK + 8)
    dump(X)


def layout(a):
    def tiled(w):
        kk, n = w.shape
        return np.ascontiguousarray(w.reshape(kk // P, P, n // P, P).transpose(2, 1, 0, 3).reshape(n // P, P, kk))

    def narrow(w):
        kk, m = w.shape
        return np.ascontiguousarray(w.reshape(kk // P, P, m).transpose(1, 0, 2).reshape(P, -1))

    def cols(v):
        return np.ascontiguousarray(v.reshape(-1, P).T)

    d = {}
    d["x"] = np.ascontiguousarray(a["x"][0].T)
    w = a["w_in"][0]
    d["w_in"] = tiled(np.concatenate([w[:, :3072], w[:, 3088:]], axis=1))
    d["w_dt"] = narrow(w[:, 3072:3088])
    d["w_branch"] = np.concatenate([tiled(a["w_branch"][0, m]) for m in range(4)])
    for name in ("lru_w_a", "lru_w_i"):
        b = np.zeros((P, 8, P), np.float32)
        b[:64, :, :64] = a[name][0, 0::2].transpose(1, 0, 2)
        b[64:, :, 64:] = a[name][0, 1::2].transpose(1, 0, 2)
        d[name] = b.reshape(P, -1)
    d["w_out"] = tiled(a["w_out"][0])
    d["ffn_up"] = tiled(a["ffn_up"][0])
    d["ffn_down"] = tiled(a["ffn_down"][0])
    d["w_mod"] = a["w_mod_2"][0]
    d["ctx"] = np.ascontiguousarray(a["ctx_2"][0].T)
    w2 = a["w_in_2"][0]
    d["w_in_2"] = tiled(np.concatenate([w2[:, :2048], w2[:, 2064:]], axis=1))
    d["w_ab"] = narrow(w2[:, 2048:2064])
    d["w_out_2"] = tiled(a["w_out_2"][0])
    d["w_router"] = narrow(a["w_router_2"][0])
    for name in ("w_gate", "w_up", "w_down"):
        d[name] = a[name + "_2"][0]
    pos, inv = np.arange(T), (10000.0 ** (-np.arange(32) / 32.0)).astype(np.float32)
    ang = np.concatenate([inv[:, None] * (pos // 64)[None], inv[:, None] * (pos // 64)[None],
                          inv[:, None] * (pos % 64)[None], inv[:, None] * (pos % 64)[None]]).astype(np.float32)
    d["cos2"], d["sin2"] = np.cos(ang), np.sin(ang)
    rpb = a["na_rpb_2"][0]
    q, kk = np.arange(64)[:, None], np.arange(64)[None, :]
    first = np.clip(q - 8, 0, 48)
    seen = (kk >= first) & (kk < first + 16)
    idx = np.clip(kk - q, -15, 15) + 15
    t = np.full((8, 64, 15, 64), np.float32(-1e38), np.float32)
    t.transpose(0, 2, 1, 3)[:, :, seen] = rpb[:, :, idx[seen]]
    d["rpb"] = t.reshape(8, 64, 15 * 64)
    d["lora_w"] = np.concatenate([a["rwkv_w2"][0], np.zeros((64, D), np.float32)])
    d["lora_a"] = np.concatenate([np.zeros((64, D), np.float32), a["rwkv_a2"][0]])
    d["lora_g"] = np.ascontiguousarray(a["rwkv_g2"][0])
    table, d["cos"], d["sin"] = ret_tables()
    d["ret_table"] = table.reshape(P, -1)
    params = np.zeros((P, NCOLS), np.float32)

    def put(name, c):
        params[:c.shape[0], COL_AT[name]:COL_AT[name] + c.shape[1]] = c

    for name, n in COLS[:31]:
        if name == "ssm_d":
            put(name, cols(np.repeat(a[name][0], 64)))
        else:
            put(name, cols(np.ascontiguousarray(a[name]).reshape(-1)))
    put("ssm_dt_bias", a["ssm_dt_bias"][0][:, None])
    put("ssm_a_log", a["ssm_a_log"][0][:, None])
    put("gdn_a_log", np.tile(a["a_log_2"].reshape(1, 8), (P, 1)))
    put("gdn_dt_bias", np.tile(a["dt_bias_2"].reshape(1, 8), (P, 1)))
    d["params"] = params
    d["consts"] = consts()
    return d


def kernel(stage="all", **inputs):
    import numpy as _np
    import concourse.bacc as _bacc
    from concourse import mybir as _mybir
    from concourse.bass_utils import run_bass_kernel_spmd as _run

    nc = _bacc.Bacc("TRN2", target_bir_lowering=False, num_devices=1)
    arrays, dr = {}, {}
    for name, v in layout({n: _np.asarray(v) for n, v in inputs.items()}).items():
        arrays[f"in_{name}"] = v
        dr[name] = nc.dram_tensor(f"in_{name}", v.shape, _mybir.dt.from_np(v.dtype), kind="ExternalInput").ap()
    dr["spill"] = nc.dram_tensor("spill", (8, P, T), _mybir.dt.float32, kind="Internal").ap()
    out = nc.dram_tensor("out_T", (D, T), _mybir.dt.float32, kind="ExternalOutput").ap()
    program(nc, dr, out, stage)
    r = _run(nc, [arrays], core_ids=[0])
    return _np.ascontiguousarray(r.results[0]["out_T"].T)[None]
```
